# Optimizing a Trainium2 kernel written in Bass

```python
import jax, jax.numpy as jnp
from jax import lax
import numpy as np

'''Hybrid streaming-encoder trunk: DEPTH layers, each with
  (1) adaLN-modulated pre-RMSNorm -> one combined input projection whose columns are split into two
      parallel head groups: a Conformer convolution group (GLU -> causal depthwise conv k=31 -> LayerNorm ->
      swish) and a chunked-attention group (QK-norm, 9-chunk band, clipped relative-position bias) ->
      concatenation -> one output projection -> gated residual;
  (2) adaLN-modulated pre-RMSNorm -> top-4-of-32 clamped-SwiGLU mixture of experts (softmax router with bias)
      -> gated residual.
Inputs: x (BATCH, SEQ, D_MODEL) float32, c (BATCH, D_MODEL) float32, plus per-layer parameters stacked on a
leading DEPTH axis. Output: (BATCH, SEQ, D_MODEL).
'''

D_MODEL = 1024
BATCH = 1
SEQ = 1024
DEPTH = 1

CHUNK = 64
D_CONV = D_MODEL // 2
D_ATTN = D_MODEL - D_CONV
N_HEADS = 8
HEAD_DIM = D_ATTN // N_HEADS
CONV_KERNEL = 31
LEFT_CHUNKS = 8
BAND_CHUNKS = LEFT_CHUNKS + 1
REL_CLIP = 128
N_EXPERTS = 32
TOP_K = 4
D_EXPERT = D_MODEL
SWIGLU_ALPHA = 1.702
SWIGLU_LIMIT = 7.0
MOE_BLOCK = 128
EPS = 1e-6
D_IN = 2 * D_CONV + 3 * D_ATTN

kernel_name = 'hybrid_conformer_chunkattn_moe_adaln'

def rms_norm(x, g):
    xf = x.astype(jnp.float32)
    y = xf * lax.rsqrt(jnp.mean(xf * xf, axis=-1, keepdims=True) + EPS)
    return (y * g).astype(x.dtype)

def layer_norm(x, g, b):
    xf = x.astype(jnp.float32)
    mu = jnp.mean(xf, axis=-1, keepdims=True)
    xc = xf - mu
    y = xc * lax.rsqrt(jnp.mean(xc * xc, axis=-1, keepdims=True) + EPS)
    return (y * g + b).astype(x.dtype)

def modulate(x, g, shift, scale):
    return rms_norm(x, g) * (1.0 + scale[:, None, :]) + shift[:, None, :]

def conv_mixer(a, gt, w, b, ln_g, ln_b):
    u = a * jax.nn.sigmoid(gt)
    y = lax.conv_general_dilated(
        u, w[:, None, :], window_strides=(1,), padding=((CONV_KERNEL - 1, 0),),
        dimension_numbers=('NWC', 'WIO', 'NWC'), feature_group_count=D_CONV) + b
    y = layer_norm(y, ln_g, ln_b)
    return jax.nn.silu(y)

def chunk_attention(q, k, v, q_g, k_g, rel_bias):
    B, S = q.shape[0], q.shape[1]
    nc = S // CHUNK
    shp = (B, nc, CHUNK, N_HEADS, HEAD_DIM)
    q = rms_norm(q.reshape(shp), q_g)
    k = rms_norm(k.reshape(shp), k_g)
    v = v.reshape(shp)
    pad = ((0, 0), (LEFT_CHUNKS, 0), (0, 0), (0, 0), (0, 0))
    band = np.arange(nc)[:, None] + np.arange(BAND_CHUNKS)[None, :]
    kb = jnp.pad(k, pad)[:, band].reshape(B, nc, BAND_CHUNKS * CHUNK, N_HEADS, HEAD_DIM)
    vb = jnp.pad(v, pad)[:, band].reshape(B, nc, BAND_CHUNKS * CHUNK, N_HEADS, HEAD_DIM)
    valid = np.repeat(band >= LEFT_CHUNKS, CHUNK, axis=1)
    dist = LEFT_CHUNKS * CHUNK + np.arange(CHUNK)[:, None] - np.arange(BAND_CHUNKS * CHUNK)[None, :]
    bias = rel_bias[:, np.clip(dist, -REL_CLIP, REL_CLIP) + REL_CLIP].astype(jnp.float32)
    s = jnp.einsum('bnqhd,bnkhd->bhnqk', q, kb, preferred_element_type=jnp.float32)
    s = s * (HEAD_DIM ** -0.5) + bias[None, :, None]
    s = jnp.where(valid[None, None, :, None, :], s, -jnp.inf)
    p = jax.nn.softmax(s, axis=-1).astype(v.dtype)
    o = jnp.einsum('bhnqk,bnkhd->bnqhd', p, vb)
    return o.reshape(B, S, D_ATTN)

def moe(h, router_w, router_b, w1, b1, w2, b2):
    B, S, D = h.shape
    T = B * S
    tk = T * TOP_K
    hf = h.reshape(T, D)
    logits = jnp.matmul(hf, router_w, preferred_element_type=jnp.float32) + router_b.astype(jnp.float32)
    top_val, top_idx = lax.top_k(logits, TOP_K)
    gates = jax.nn.softmax(top_val, axis=-1)
    e = top_idx.reshape(-1).astype(jnp.int32)
    tok = jnp.arange(tk, dtype=jnp.int32) // TOP_K
    gw = gates.reshape(-1)
    order = jnp.argsort(e)
    e_s = e[order]
    counts = jnp.bincount(e, length=N_EXPERTS).astype(jnp.int32)
    starts = jnp.cumsum(counts) - counts
    pad_counts = (counts + MOE_BLOCK - 1) // MOE_BLOCK * MOE_BLOCK
    pad_ends = jnp.cumsum(pad_counts)
    pad_starts = pad_ends - pad_counts
    dest = pad_starts[e_s] + (jnp.arange(tk, dtype=jnp.int32) - starts[e_s])
    n_slots = -(-tk // MOE_BLOCK) * MOE_BLOCK + N_EXPERTS * MOE_BLOCK
    n_blocks = n_slots // MOE_BLOCK
    slot_tok = jnp.full((n_slots,), T, jnp.int32).at[dest].set(tok[order])
    slot_w = jnp.zeros((n_slots,), jnp.float32).at[dest].set(gw[order])
    block_exp = jnp.minimum(
        jnp.searchsorted(pad_ends, jnp.arange(n_blocks, dtype=jnp.int32) * MOE_BLOCK, side='right'),
        N_EXPERTS - 1)
    h_pad = jnp.concatenate([hf, jnp.zeros((1, D), hf.dtype)], axis=0)
    xb = h_pad[slot_tok].reshape(n_blocks, MOE_BLOCK, D)

    def expert_block(args):
        xs, ei = args
        u = xs @ w1[ei] + b1[ei]
        glu, lin = u[:, :D_EXPERT], u[:, D_EXPERT:]
        glu = jnp.minimum(glu, SWIGLU_LIMIT)
        lin = jnp.clip(lin, -SWIGLU_LIMIT, SWIGLU_LIMIT)
        act = glu * jax.nn.sigmoid(SWIGLU_ALPHA * glu) * (lin + 1.0)
        return act @ w2[ei] + b2[ei]

    yb = lax.map(expert_block, (xb, block_exp)).reshape(n_slots, D)
    y = jnp.zeros((T + 1, D), h.dtype).at[slot_tok].add(yb * slot_w[:, None].astype(h.dtype))
    return y[:T].reshape(B, S, D)

def setup_inputs(seed: int = 0) -> dict:
    key = jax.random.key(seed)
    ks = jax.random.split(key, 24)

    def nrm(k, shape, scale):
        return scale * jax.random.normal(k, shape, jnp.float32)

    d = D_MODEL
    return {
        'x': nrm(ks[0], (BATCH, SEQ, d), 1.0),
        'c': nrm(ks[1], (BATCH, d), 1.0),
        'ada_w': nrm(ks[2], (DEPTH, d, 6 * d), 0.5 * d ** -0.5),
        'ada_b': nrm(ks[3], (DEPTH, 6 * d), 0.02),
        'norm1_g': 1.0 + nrm(ks[4], (DEPTH, d), 0.02),
        'w_in': nrm(ks[5], (DEPTH, d, D_IN), d ** -0.5),
        'conv_w': nrm(ks[6], (DEPTH, CONV_KERNEL, D_CONV), CONV_KERNEL ** -0.5),
        'conv_b': nrm(ks[7], (DEPTH, D_CONV), 0.02),
        'conv_ln_g': 1.0 + nrm(ks[8], (DEPTH, D_CONV), 0.02),
        'conv_ln_b': nrm(ks[9], (DEPTH, D_CONV), 0.02),
        'q_norm_g': 1.0 + nrm(ks[10], (DEPTH, HEAD_DIM), 0.02),
        'k_norm_g': 1.0 + nrm(ks[11], (DEPTH, HEAD_DIM), 0.02),
        'rel_bias': nrm(ks[12], (DEPTH, N_HEADS, 2 * REL_CLIP + 1), 0.1),
        'w_out': nrm(ks[13], (DEPTH, d, d), d ** -0.5),
        'norm2_g': 1.0 + nrm(ks[14], (DEPTH, d), 0.02),
        'router_w': nrm(ks[15], (DEPTH, d, N_EXPERTS), d ** -0.5),
        'router_b': nrm(ks[16], (DEPTH, N_EXPERTS), 0.01),
        'exp_w1': nrm(ks[17], (DEPTH, N_EXPERTS, d, 2 * D_EXPERT), d ** -0.5),
        'exp_b1': nrm(ks[18], (DEPTH, N_EXPERTS, 2 * D_EXPERT), 0.02),
        'exp_w2': nrm(ks[19], (DEPTH, N_EXPERTS, D_EXPERT, d), D_EXPERT ** -0.5),
        'exp_b2': nrm(ks[20], (DEPTH, N_EXPERTS, d), 0.02),
    }

def reference(x, c, ada_w, ada_b, norm1_g, w_in, conv_w, conv_b, conv_ln_g, conv_ln_b,
              q_norm_g, k_norm_g, rel_bias, w_out, norm2_g, router_w, router_b,
              exp_w1, exp_b1, exp_w2, exp_b2):
    c_act = jax.nn.silu(c)
    split_pts = [D_CONV, 2 * D_CONV, 2 * D_CONV + D_ATTN, 2 * D_CONV + 2 * D_ATTN]
    for l in range(DEPTH):
        mod = c_act @ ada_w[l] + ada_b[l]
        sh1, sc1, g1, sh2, sc2, g2 = jnp.split(mod, 6, axis=-1)
        h = modulate(x, norm1_g[l], sh1, sc1)
        u = h @ w_in[l]
        a, gt, q, k, v = jnp.split(u, split_pts, axis=-1)
        y_conv = conv_mixer(a, gt, conv_w[l], conv_b[l], conv_ln_g[l], conv_ln_b[l])
        y_attn = chunk_attention(q, k, v, q_norm_g[l], k_norm_g[l], rel_bias[l])
        mixed = jnp.concatenate([y_conv, y_attn], axis=-1) @ w_out[l]
        x = x + g1[:, None, :] * mixed
        h2 = modulate(x, norm2_g[l], sh2, sc2)
        y_moe = moe(h2, router_w[l], router_b[l], exp_w1[l], exp_b1[l], exp_w2[l], exp_b2[l])
        x = x + g2[:, None, :] * y_moe
    return x


_drawn_inputs = setup_inputs


def setup_inputs(seed=0):
    import zlib

    import numpy as np

    out = dict(_drawn_inputs(seed))
    spreads = {}
    factors = {'norm1_g': 8.0,
     'conv_b': 6.905,
     'conv_ln_g': 22.209,
     'conv_ln_b': 20.431,
     'q_norm_g': 8.0,
     'k_norm_g': 8.0,
     'rel_bias': 8.0,
     'norm2_g': 3.579,
     'router_b': 17.892,
     'exp_b1': 8.0,
     'exp_b2': 37.864}
    for name, (base, spread) in spreads.items():
        noise = np.random.default_rng([zlib.crc32(name.encode()), seed]).standard_normal(out[name].shape)
        drawn = base * np.exp(spread * noise) if base else spread * noise
        out[name] = __import__('jax').numpy.asarray(drawn.astype(out[name].dtype))
    for name, factor in factors.items():
        out[name] = (out[name] * factor).astype(out[name].dtype)
    return out
```

```python
from contextlib import ExitStack

import concourse.bass as bass
from concourse import mybir

F32 = mybir.dt.float32
F32R = mybir.dt.float32r
I32 = mybir.dt.int32
U32 = mybir.dt.uint32
ACT = mybir.ActivationFunctionType
ALU = mybir.AluOpType
AX_X = mybir.AxisListType.X

P = 128
T = 1024
D = 1024
TT = T // P
KT = D // P
CW = 512
CT = 512 // P
KC = 31
NH, HD = 8, 64
E = 32
TOPK = 4
MAXB = 4
SPLITS = T // (MAXB * P)
CAND = E * SPLITS
TABW = 44
EPS = 1e-6
NEG = -1e30
ALPHA, LIMIT = 1.702, 7.0
A_CH, GT_CH, K_CH, V_CH, Q_CH, O_CH, X_CH = 0, 1, 2, 3, 4, 5, 7
W_IN_COL = [0, 512, 1536, 2048, 1024]
NPC = 6
V_KT = 5
SQ = 256

C_ID, C_ONE, C_COL, C_FAR, C_NEAR = 0, 128, 256, 272, 656
C_TRI, C_STRI, C_RM1, C_THR, C_VAL, C_IOTA = 912, 1040, 1104, 1148, 1152, 1154
N_CONST = C_IOTA + P
V_C, V_G1, V_ADA, V_CB, V_LG, V_LB, N_VEC = 0, 8, 16, 32, 36, 40, 44


def make_consts():
    import numpy as np
    c = np.zeros((P, N_CONST), np.float32)
    p = np.arange(P)
    c[:, C_ID:C_ID + P] = np.eye(P)
    c[:, C_ONE:C_ONE + P] = 1
    c[:, C_COL:C_COL + 8] = p[:, None] + P * np.arange(8)
    c[:, C_COL + 8] = T + p
    c[:, C_COL + 9] = -(T + p)
    c[:, C_COL + 10] = EPS
    c[:, C_COL + 11] = HD * EPS
    c[64:, C_FAR:C_FAR + 64] = NEG
    c[:64, C_NEAR:C_NEAR + 64] = NEG
    c[:, C_TRI:C_TRI + P] = p[:, None] <= p[None, :]
    c[:64, C_STRI:C_STRI + 64] = p[:64, None] < p[None, :64]
    c[:, C_RM1:C_RM1 + TABW] = np.arange(TABW) - 1
    c[:, C_THR:C_THR + MAXB] = MAXB * P * (p % SPLITS)[:, None] + P * np.arange(MAXB)
    c[:, C_VAL] = p // SPLITS
    c[:, C_VAL + 1] = MAXB * P * (p % SPLITS)
    c[:, C_IOTA:] = np.arange(P)
    return c


def layer(nc, x, c, ada_w, ada_b, norm1_g, w_in, conv_w, conv_b, ln_g, ln_b, q_g, k_g, rel_bias, w_out,
          norm2_g, router_w, router_b, w1, b1, w2, b2, consts, rel_ext, mod_dram, h2_dram, out):
    with ExitStack() as ctx:
        base = (nc.sbuf_base + 31) // 32 * 32
        KB = 1024

        def size(shape):
            n = 4
            for s in shape[1:]:
                n *= s
            return n

        def at(name, shape, off, dt=F32):
            assert off % 32 == 0 and base + off + size(shape) <= nc.sbuf_usable_end, (name, off + size(shape))
            return nc.alloc_sbuf_tensor_at(name, shape, dt, offset=base + off)

        def sem(name):
            return ctx.enter_context(nc.semaphore(name))

        def view(ap, dims, offset=0):
            return bass.AP(ap.tensor, ap.offset + offset, [list(ap.ap[0])] + dims)

        OPND, WORK = 96 * KB, 160 * KB
        TAB = WORK + 37376
        SMALL = TAB + 8 * KB
        stage = [at("stage0", [P, KT, CW], 0), at("stage1", [P, KT, CW], 16 * KB)]
        w_hi = [at("w_hi0", [P, KT, CW], 32 * KB, F32R), at("w_hi1", [P, KT, CW], 64 * KB, F32R)]
        w_lo = [at("w_lo0", [P, KT, CW], 48 * KB, F32R), at("w_lo1", [P, KT, CW], 80 * KB, F32R)]
        cst = at("cst", [P, C_FAR], SMALL)
        ident, ones = cst[:, C_ID:C_ID + P], cst[:, C_ONE:C_ONE + P]
        tok_id = cst[:, C_COL:C_COL + 8]
        pad_id, neg_pad = cst[:, C_COL + 8:C_COL + 9], cst[:, C_COL + 9:C_COL + 10]
        eps_col, eps64_col = cst[:, C_COL + 10:C_COL + 11], cst[:, C_COL + 11:C_COL + 12]
        spot = [SMALL + 4 * C_FAR]

        def tiny(name, shape, dt=F32):
            t = at(name, shape, spot[0], dt)
            spot[0] += (size(shape) + 31) // 32 * 32
            return t

        x_rows = at("x_rows", [P, TT, D], 64 * KB)
        ada_t = [at("ada0", [P, 2048], 16 * KB), at("ada1", [P, 2048], 24 * KB)]
        ada_acc = at("ada_acc", [P, 2048], WORK + 16896)
        mod_row = at("mod_row", [1, 2048], WORK + 16896 + 8 * KB)
        h_full = [at("h_full0", [P, T], WORK), at("h_full1", [P, T], WORK + 4 * KB)]
        op_hi = at("op_hi", [P, KT, T], OPND, F32R)
        op_lo = at("op_lo", [P, KT, T], OPND + 32 * KB, F32R)
        uT = at("uT", [P, CT, KC - 1 + T], WORK)
        kT = at("kT", [P, 4, T], WORK + 16896)
        acc = at("acc", [P, T], WORK + 33280)
        sig_t = [at("sig_t0", [P, CW], WORK + 33280), at("sig_t1", [P, CW], WORK + 35328)]
        v_rows = at("v_rows", [P, TT, 512], 16 * KB)
        k_sq = at("k_sq", [P, 512], 16 * KB)
        k_row = at("k_row", [P, 512], 18 * KB)
        qT = at("qT", [P, KT, T], OPND)
        q_tmp = at("q_tmp", [P, KT, T], OPND + 32 * KB)
        rel_rows = at("rel_rows", [NH, 384], TAB)
        vec_rows = at("vec_rows", [N_VEC, P], TAB + 2 * KB)
        tap_rows = at("tap_rows", [KC, 512], TAB + 4 * KB)
        near_bias = at("near_bias", [P, NH, 256], TAB)
        s_sb = [at(f"s_sb{i}", [P, 640], OPND + 32 * KB + 2560 * i) for i in range(2)]
        p_T = [at(f"p_T{i}", [P, 640], OPND + 37 * KB + 2560 * i) for i in range(2)]
        y_row = at("y_row", [P, 512], OPND + 42 * KB)
        masks = at("masks", [P, 640], OPND + 44 * KB)
        taps = tiny("taps", [P, CT, KC])
        gains = tiny("gains", [P, 2, HD])
        stat = tiny("stat", [P, 16])
        sq_sum = tiny("sq_sum", [P, 8])
        sq_root = tiny("sq_root", [P, 8])
        sq_inv = tiny("sq_inv", [P, 8])
        mx = tiny("mx", [P, 8])
        rsum = tiny("rsum", [P, 16])
        r_inv = tiny("r_inv", [P, 8])
        cols = tiny("cols", [P, N_VEC])
        c_act = tiny("c_act", [P, 16])
        mod_col = tiny("mod_col", [P, 16])
        ln_a = at("ln_a", [P, T], 16 * KB)
        ln_t = at("ln_t", [P, T], 20 * KB)
        ln_r = at("ln_r", [P, T], 24 * KB)
        ln_z = at("ln_z", [P, T], 28 * KB)
        ln_sq = lambda t: (ln_a, ln_t)[t % 2]
        ln_sig = lambda t: (ln_z, ln_a)[t % 2]
        x2 = at("x2", [P, TT, D], WORK)
        g1_row = at("g1_row", [P, D], 16 * KB)
        a2_row = at("a2_row", [P, D], 20 * KB)
        sh2_row = at("sh2_row", [P, D], 24 * KB)
        t_row = [at("t_row0", [P, CW], 28 * KB), at("t_row1", [P, CW], 30 * KB)]
        h2r = at("h2r", [P, KT, T], OPND)
        h2T = at("h2T", [P, KT, T], OPND + 32 * KB)
        rw = at("rw", [P, KT, E], WORK + 32 * KB)
        rb_row = at("rb_row", [P, E], WORK + 33 * KB)
        n2_row = at("n2_row", [P, D], TAB + 4 * KB)
        R = OPND
        lgt = at("lgt", [P, TT, E], WORK + 33 * KB + 128)
        top = at("top", [P, TT, 8], WORK + 34 * KB + 128)
        top_i = at("top_i", [P, TT, 8], WORK + 34 * KB + 384, U32)
        top_f = at("top_f", [P, TT, 8], WORK + 34 * KB + 640)
        consts2 = at("consts2", [P, C_IOTA - C_TRI], R)
        tri = consts2[:, 0:P]
        stri = consts2[0:CAND, C_STRI - C_TRI:C_STRI - C_TRI + CAND]
        row_m1 = consts2[0:CAND, C_RM1 - C_TRI:C_RM1 - C_TRI + TABW]
        thr = consts2[0:CAND, C_THR - C_TRI:C_THR - C_TRI + MAXB]
        cand_val = consts2[0:CAND, C_VAL - C_TRI:C_VAL - C_TRI + 2]
        gex = at("gex", [P, TT, TOPK], R + 2 * KB)
        gsum = at("gsum", [P, TT], R + 2 * KB + 128)
        nmax = at("nmax", [P, TT], R + 2 * KB + 160)
        ginv = at("ginv", [P, TT], R + 2 * KB + 192)
        hot = at("hot", [P, TT, E], R + 3 * KB)
        hotg = at("hotg", [P, TT, E], R + 4 * KB)
        mask = at("mask", [P, TT, E], R + 5 * KB)
        gate_te = at("gate_te", [P, TT, E], R + 6 * KB)
        rank = at("rank", [P, TT, E], R + 7 * KB)
        pre = at("pre", [P, TT, E], R + 8 * KB)
        mask2 = at("mask2", [P, TT, CAND], R + 14 * KB)
        cmp = at("cmp", [CAND, MAXB], R + 9 * KB)
        cand = at("cand", [CAND, 8], R + 9 * KB + 32)
        sel = at("sel", [CAND, TABW], R + 10 * KB)
        base_rep = at("base_rep", [CAND, P], R + 11 * KB)
        xT_hi = [at(f"xT_hi{b}", [P, KT, P], OPND + 4 * KB * b, F32R) for b in range(MAXB)]
        xT_lo = [at(f"xT_lo{b}", [P, KT, P], OPND + 16 * KB + 4 * KB * b, F32R) for b in range(MAXB)]
        aT_hi = [at(f"aT_hi{b}", [P, KT, P], OPND + 32 * KB + 4 * KB * b, F32R) for b in range(MAXB)]
        aT_lo = [at(f"aT_lo{b}", [P, KT, P], OPND + 48 * KB + 4 * KB * b, F32R) for b in range(MAXB)]
        xg = [at(f"xg{b}", [P, D], WORK + 4 * KB * b) for b in range(MAXB)]
        yst = [at(f"yst{b}", [P, CW], WORK + 16 * KB + 2 * KB * b) for b in range(2)]
        bias = [at(f"bias{b}", [P, CW], WORK + 20 * KB + 2 * KB * b) for b in range(3)]
        onehot = at("onehot", [P, TT, P], WORK + 26 * KB, F32R)
        ut = at("ut", [P, CW], WORK + 30 * KB)
        sg = at("sg", [P, SQ], WORK + 32 * KB)
        act_r = [at(f"act_r{b}", [P, SQ], WORK + 33 * KB + KB * b) for b in range(3)]
        g2_row = at("g2_row", [P, D], TAB)
        pos_et = at("pos_et", [P, E, TT], TAB + 4 * KB)
        gate_et = at("gate_et", [P, E, TT], TAB + 5 * KB)
        iota = at("iota", [P, P], TAB + 6 * KB)
        act_r.append(at("act_r3", [P, SQ], TAB + 6 * KB + 512))
        spot[0] = SMALL + 4 * C_FAR
        tab = tiny("tab", [1, 5 * TABW], I32)
        pbase = tiny("pbase", [P, TABW])
        posr = tiny("posr", [P, TT])
        posb = tiny("posb", [P, TT])
        rhs = tiny("rhs", [P, TT, 4], F32R)
        gcur = tiny("gcur", [P, TT])
        g_idx = tiny("g_idx", [P, MAXB], U32)
        s_nxt = tiny("s_nxt", [P, 2, MAXB], U32)
        s_cur = tiny("s_cur", [P, 2, MAXB], U32)
        gt_nxt = tiny("gt_nxt", [P, MAXB])
        gt_cur = tiny("gt_cur", [P, MAXB])
        s_tmp = tiny("s_tmp", [P, MAXB])
        i_sb = tiny("i_sb", [P, 4])

        pair = [ctx.enter_context(nc.psum_tensor(f"pair{i}", [P, 2 * CW], F32)) for i in range(4)]

        def bank(i):
            return pair[i // 2][:, i % 2 * CW:(i % 2 + 1) * CW]

        s_cst, s_vec, s_tap, s_relrow, s_gain = (sem(n) for n in ("s_cst", "s_vec", "s_tap", "s_relrow", "s_gain"))
        s_x = [sem("s_x0"), sem("s_x1")]
        s_ada = [sem("s_ada0"), sem("s_ada1")]
        s_adab = sem("s_adab")
        s_stage = [sem("s_stage0"), sem("s_stage1")]
        s_hi, s_lo, s_plo = sem("s_hi"), sem("s_lo"), sem("s_plo")
        s_vecT, s_cols, s_csig, s_cact = sem("s_vecT"), sem("s_cols"), sem("s_csig"), sem("s_cact")
        s_tapT, s_taps = sem("s_tapT"), sem("s_taps")
        s_ssq, s_xroot, s_xn = sem("s_ssq"), sem("s_xroot"), sem("s_xn")
        s_adastep, s_modp, s_modc, s_modr, s_modst = (sem(n) for n in ("s_adastep", "s_modp", "s_modc", "s_modr", "s_modst"))
        s_modfree = sem("s_modfree")
        s_xT, s_hfull, s_hhi, s_hlo = sem("s_xT"), sem("s_hfull"), sem("s_hhi"), sem("s_hlo")
        s_tile, s_tfree = sem("s_tile"), sem("s_tfree")
        s_gsig, s_uz = sem("s_gsig"), sem("s_uz")
        s_qsq, s_qss, s_qroot, s_qn, s_qkT, s_qkev = (sem(n) for n in ("s_qsq", "s_qss", "s_qroot", "s_qn", "s_qkT", "s_qkev"))
        s_dve = sem("s_dve")
        s_relst, s_relld, s_near, s_mask = sem("s_relst"), sem("s_relld"), sem("s_near"), sem("s_mask")
        s_rel = sem("s_rel")
        s_S, s_Sfree, s_nmx, s_exp, s_PT, s_pTc, s_PV, s_y, s_yT, s_yhi, s_ylo = (
            sem(n) for n in ("s_S", "s_Sfree", "s_nmx", "s_exp", "s_PT", "s_pTc", "s_PV", "s_y", "s_yT", "s_yhi", "s_ylo"))
        s_lnsum, s_lnc, s_lnsq, s_lnvar, s_lnroot, s_lnz, s_lnsig, s_lny, s_lnhi, s_lnlo = (
            sem(n) for n in ("s_lnsum", "s_lnc", "s_lnsq", "s_lnvar", "s_lnroot", "s_lnz", "s_lnsig", "s_lny", "s_lnhi", "s_lnlo"))
        s_x2ld, s_rows, s_g2 = sem("s_x2ld"), sem("s_rows"), sem("s_g2")
        s_x2, s_x2sq, s_x2root, s_h2, s_h2T, s_h2Tc, s_lg = (
            sem(n) for n in ("s_x2", "s_x2sq", "s_x2root", "s_h2", "s_h2T", "s_h2Tc", "s_lg"))
        s_a2, s_h2st, s_outst, s_c2 = sem("s_a2"), sem("s_h2st"), sem("s_outst"), sem("s_c2")
        s_nm, s_gex, s_mk, s_rk, s_cn, s_cv, s_pf, s_sl, s_tb, s_tab, s_iota = (
            sem(n) for n in ("s_nm", "s_gex", "s_mk", "s_rk", "s_cn", "s_cv", "s_pf", "s_sl", "s_tb", "s_tab", "s_iota"))
        m_done = sem("m_done")
        m_free = sem("m_free")
        glu_ok, sig_ok, act_ok = sem("glu_ok"), sem("sig_ok"), sem("act_ok")
        aT_ps, aT_h, aT_l = sem("aT_ps"), sem("aT_h"), sem("aT_l")
        oh_ok, i_ps, idx_ok = sem("oh_ok"), sem("i_ps"), sem("idx_ok")
        g_in, x_ps, x_h, x_l = sem("g_in"), sem("x_ps"), sem("x_h"), sem("x_l")
        g_go, y_go = sem("g_go"), sem("y_go")
        y_ok, y_out = sem("y_ok"), sem("y_out")
        s_bias = [sem(f"s_bias{i}") for i in range(3)]

        w_in_v = w_in.rearrange("(k p) n -> p k n", p=P)
        w_out_v = w_out.rearrange("(k p) n -> p k n", p=P)
        w1_v = w1.rearrange("e (k p) (s n) -> e p k s n", p=P, s=2)
        w2_v = w2.rearrange("e (k p) n -> e p k n", p=P)
        out_half = out.rearrange("t (h n) -> (t h) n", h=2)
        u_bank = [(0, 1), (2, 2), (3, 3), (4, 4)]
        N_QK = 2 * TT

        def write_hi(act, par, slot, seen):
            act.wait_ge(s_stage[slot], seen)
            act.activation(w_hi[par][:], stage[slot][:], ACT.Copy).then_inc(s_hi, 1)

        def write_lo(eng, par, slot, number, tiles, done):
            eng.wait_ge(s_hi, number)
            eng.tensor_tensor(w_lo[par][:, tiles, :], stage[slot][:, tiles, :], w_hi[par][:, tiles, :].bitcast(F32),
                              ALU.subtract).then_inc(done, 1)

        def before_trunk_split(eng, C):
            if C == 1:
                eng.wait_ge(s_xT, KT)
            elif C >= 2:
                eng.wait_ge(s_tile, 8 * (C - 1))

        block = ctx.enter_context(nc.Block())

        @block.sync
        def _(sp):
            sp.dma_start(cst[:], consts[:, 0:C_FAR]).then_inc(s_cst, 16)
            sp.dma_start(vec_rows[V_C:V_C + 8, :], c.rearrange("a (k p) -> (a k) p", p=P)).then_inc(s_vec, 16)
            sp.dma_start(vec_rows[V_G1:V_G1 + 8, :], norm1_g.rearrange("(k p) -> k p", p=P)).then_inc(s_vec, 16)
            sp.dma_start(vec_rows[V_ADA:V_ADA + 16, :], ada_b[0:2048].rearrange("(k p) -> k p", p=P)).then_inc(s_vec, 16)
            for v, n in ((conv_b, V_CB), (ln_g, V_LG), (ln_b, V_LB)):
                sp.dma_start(vec_rows[n:n + 4, :], v.rearrange("(k p) -> k p", p=P)).then_inc(s_vec, 16)
            sp.dma_start(tap_rows[:], conv_w).then_inc(s_tap, 16)
            xv = x.rearrange("(i p) d -> p i d", p=P)
            for h in range(2):
                sp.dma_start(x_rows[:, 4 * h:4 * h + 4, :], xv[:, 4 * h:4 * h + 4, :]).then_inc(s_x[h], 16)
            sp.dma_start(stage[0][:], w_in_v[:, :, 0:CW]).then_inc(s_stage[0], 16)
            sp.dma_start(rel_rows[:, 0:257], rel_bias).then_inc(s_relrow, 16)
            sp.dma_start(gains[:, 0, :], q_g.partition_broadcast(P)).then_inc(s_gain, 16)
            sp.dma_start(gains[:, 1, :], k_g.partition_broadcast(P)).then_inc(s_gain, 16)
            sp.wait_ge(s_rel, 1)
            sp.dma_start(rel_ext, rel_rows[:]).then_inc(s_relst, 16)

            def load_chunk(C):
                sp.wait_ge(s_hi, C)
                sp.wait_ge(s_lo, C)
                sp.wait_ge(s_plo, C)
                src = w_in_v[:, :, W_IN_COL[C]:W_IN_COL[C] + CW] if C < O_CH else w_out_v[:, :, (C - O_CH) * CW:(C - O_CH + 1) * CW]
                sp.dma_start(stage[0][:], src).then_inc(s_stage[0], 16)

            load_chunk(1)
            sp.wait_ge(s_relst, 16)
            sp.wait_ge(s_cols, 1)
            sp.wait_ge(s_taps, 1)
            for h in range(NH):
                sp.dma_start(near_bias[:, h, :], bass.AP(rel_ext.tensor, rel_ext.offset + 384 * h + 1, [[1, P], [1, 256]])).then_inc(s_relld, 16)
            load_chunk(2)
            for half in range(2):
                sp.wait_ge(s_modr, half + 1)
                sp.dma_start(mod_dram[2048 * half:2048 * half + 2048].rearrange("(a n) -> a n", a=1), mod_row[:]).then_inc(s_modst, 16)
            load_chunk(3)
            load_chunk(4)
            load_chunk(5)
            sp.wait_ge(s_tile, 8 * 5)
            sp.wait_ge(s_qkT, N_QK)
            sp.dma_start(masks[:], consts[:, C_FAR:C_FAR + 640]).then_inc(s_mask, 16)
            sp.wait_ge(s_modst, 32)
            sp.wait_ge(s_lnhi, CT)
            sp.wait_ge(s_lnlo, CT)
            sp.wait_ge(s_ylo, TT)
            xv2 = x.rearrange("(i p) d -> p i d", p=P)
            sp.dma_start(x2[:], xv2).then_inc(s_x2ld, 16)
            sp.dma_start(g1_row[:], mod_dram[0:1024].partition_broadcast(P)).then_inc(s_rows, 16)
            sp.dma_start(sh2_row[:], mod_dram[1024:2048].partition_broadcast(P)).then_inc(s_rows, 16)
            sp.dma_start(a2_row[:], mod_dram[2048:3072].partition_broadcast(P)).then_inc(s_rows, 16)
            sp.dma_start(n2_row[:], norm2_g.partition_broadcast(P)).then_inc(s_rows, 16)
            sp.dma_start(g2_row[:], mod_dram[3072:4096].partition_broadcast(P)).then_inc(s_rows, 16)
            sp.dma_start(rw[:], router_w.rearrange("(k p) e -> p k e", p=P)).then_inc(s_rows, 16)
            sp.dma_start(rb_row[:], router_b.partition_broadcast(P)).then_inc(s_rows, 16)
            load_chunk(6)
            for i in range(TT):
                sp.wait_ge(s_h2, i + 1)
                sp.dma_start(out[i * P:(i + 1) * P, :], x2[:, i, :]).then_inc(s_outst, 16)
                sp.dma_start(h2_dram[i * P:(i + 1) * P, :].rearrange("p (k f) -> p k f", f=P),
                             h2r[:, :, i * P:(i + 1) * P]).then_inc(s_h2st, 16)
            sp.wait_ge(s_lg, TT)
            sp.wait_ge(s_h2st, 16 * TT)
            sp.wait_ge(s_tile, 8 * X_CH)
            sp.dma_start(consts2[:], consts[:, C_TRI:C_IOTA]).then_inc(s_c2, 16)
            sp.dma_start(iota[:], consts[:, C_IOTA:C_IOTA + P]).then_inc(s_iota, 16)

            sp.wait_ge(s_tab, 1)
            passes = sp.value_load(tab[0:1, 4 * TABW:4 * TABW + 1], min_val=1, max_val=TABW - 2)
            with sp.Fori(0, passes) as p:
                ex = sp.value_load(tab[0:1, bass.ds(p + 1, 1)], min_val=0, max_val=E - 1)
                n = sp.value_load(tab[0:1, bass.ds(p + (TABW + 1), 1)], min_val=1, max_val=MAXB)
                n_p = sp.value_load(tab[0:1, bass.ds(p + TABW, 1)], min_val=0, max_val=MAXB)
                B = sp.value_load(tab[0:1, bass.ds(p + (2 * TABW + 1), 1)], min_val=0, max_val=64)
                w0 = sp.value_load(tab[0:1, bass.ds(p + 3 * TABW, 1)], min_val=0, max_val=512)

                def weights(c):
                    slot = (X_CH + c) % 2
                    sp.wait_ge(s_hi, p * NPC + (X_CH + c - 1))
                    sp.wait_ge(s_lo, p * NPC + (X_CH + c - 1))
                    sp.wait_ge(s_plo, p * NPC + (X_CH + c - 1))
                    if c < 4:
                        for s in range(2):
                            sp.dma_start(stage[slot][:, :, s * SQ:(s + 1) * SQ],
                                         w1_v[bass.ds(ex, 1), :, :, s, c * SQ:(c + 1) * SQ].rearrange("e p k n -> (e p) k n")
                                         ).then_inc(s_stage[slot], 16)
                    else:
                        sp.dma_start(stage[slot][:], w2_v[bass.ds(ex, 1), :, :, (c - 4) * CW:(c - 3) * CW].rearrange("e p k n -> (e p) k n")
                                     ).then_inc(s_stage[slot], 16)

                def biases(c):
                    if c >= 3:
                        sp.wait_ge(m_free, B * NPC + n * (c - 2) + 2)
                    else:
                        sp.wait_ge(m_free, w0 + n_p * c + 1)
                    if c < 4:
                        for s in range(2):
                            sp.dma_start(bias[(X_CH + c) % 3][:, s * SQ:(s + 1) * SQ],
                                         b1[bass.ds(ex, 1), s * D + c * SQ:s * D + (c + 1) * SQ].to_broadcast([P, SQ])
                                         ).then_inc(s_bias[(X_CH + c) % 3], 16)
                    else:
                        sp.dma_start(bias[(X_CH + c) % 3][:], b2[bass.ds(ex, 1), (c - 4) * CW:(c - 3) * CW].to_broadcast([P, CW])
                                     ).then_inc(s_bias[(X_CH + c) % 3], 16)

                weights(0)
                for c_ in range(1, NPC):
                    weights(c_)
                    biases(c_ - 1)
                biases(NPC - 1)
            sp.wait_ge(s_outst, 16 * TT)

        @block.gpsimd
        def _(pool):
            def ada_loads(part):
                for k in range(KT):
                    n = part * KT + k
                    if n >= 2:
                        pool.wait_ge(s_adastep, n - 1)
                    pool.dma_start(ada_t[n % 2][:], ada_w[k * P:(k + 1) * P, part * 2048:(part + 1) * 2048]
                                   ).then_inc(s_ada[n % 2], 16)

            def lo_part(C):
                before_trunk_split(pool, C)
                write_lo(pool, C % 2, 0, C + 1, slice(V_KT, KT), s_plo)

            ada_loads(0)
            lo_part(0)
            lo_part(1)
            pool.dma_start(mod_row[:], ada_b[2048:4096].rearrange("(a n) -> a n", a=1)).then_inc(s_adab, 16)
            ada_loads(1)
            lo_part(2)
            pool.wait_ge(s_modst, 16)
            pool.dma_start(mod_row[:], ada_b[4096:6144].rearrange("(a n) -> a n", a=1)).then_inc(s_adab, 16)
            ada_loads(2)
            lo_part(3)
            lo_part(4)
            lo_part(5)
            lo_part(6)
            pool.wait_ge(s_h2, 1)
            pool.dma_start(out[T:T + P, :], x2[:, 0, :]).then_inc(y_out, 16)
            pool.wait_ge(s_tab, 1)
            pool.wait_ge(s_h2st, 16 * TT)
            pool.wait_ge(s_outst, 16 * TT)

            def gather(b, ix, first, B=None, n=None):
                pool.wait_ge(idx_ok, ix + 1)
                if not first or b:
                    pool.wait_ge(g_in, 16 * ix if first else ix * 16)
                if not first:
                    pool.wait_ge(x_ps, B * 2 + n * 2)
                pool.sem_inc(g_go, 1)
                pool.indirect_dma_start(xg[b][:], None, h2_dram, bass.IndirectOffsetOnAxis(ap=g_idx[:, b:b + 1], axis=0)
                                        ).then_inc(g_in, 16)

            def lo_of(par, slot, number):
                write_lo(pool, par, slot, number, slice(V_KT, KT), s_plo)

            passes = pool.value_load(tab[0:1, 4 * TABW:4 * TABW + 1], min_val=1, max_val=TABW - 2)
            n0 = pool.value_load(tab[0:1, TABW + 1:TABW + 2], min_val=1, max_val=MAXB)
            lo_of(X_CH % 2, X_CH % 2, X_CH + 1)
            for b in range(MAXB):
                if b:
                    with pool.If(n0 > b):
                        gather(b, b, True)
                else:
                    gather(b, b, True)
            with pool.Fori(0, passes) as p:
                n = pool.value_load(tab[0:1, bass.ds(p + (TABW + 1), 1)], min_val=1, max_val=MAXB)
                n2 = pool.value_load(tab[0:1, bass.ds(p + (TABW + 2), 1)], min_val=0, max_val=MAXB)
                B = pool.value_load(tab[0:1, bass.ds(p + (2 * TABW + 1), 1)], min_val=0, max_val=64)
                for c_ in range(NPC):
                    def next_lo():
                        pool.wait_ge(m_done, B * NPC + n * c_ + 1)
                        lo_of((X_CH + c_ + 1) % 2, (X_CH + c_ + 1) % 2, p * NPC + (X_CH + c_ + 2))
                    if c_ < NPC - 1:
                        next_lo()
                    else:
                        with pool.If(n2 > 0):
                            next_lo()
                    if c_ >= 2:
                        with pool.If(n2 > c_ - 2):
                            gather(c_ - 2, B + n + (c_ - 2), False, B, n)
                    if c_ >= 4:
                        for b in range(MAXB):
                            def scatter():
                                iy = B * 2 + n * (c_ - 4) + b
                                pool.wait_ge(y_ok, iy + 1)
                                pool.wait_ge(y_out, iy * 16 + 16)
                                pool.sem_inc(y_go, 1)
                                pool.indirect_dma_start(
                                    out_half, bass.IndirectOffsetOnAxis(ap=s_cur[:, c_ - 4, b:b + 1], axis=0),
                                    yst[(b + c_) % 2][:], None, compute_op=ALU.add).then_inc(y_out, 16)
                            if b:
                                with pool.If(n > b):
                                    scatter()
                            else:
                                scatter()
            end = pool.value_load(tab[0:1, 4 * TABW + 1:4 * TABW + 2], min_val=1, max_val=256)
            pool.wait_ge(y_out, end * 32 + 16)

        @block.tensor
        def _(pe):
            def product(dst, a_hi, a_lo, b_hi, b_lo, kts, start, stop):
                for k in kts:
                    for i, (u, v) in enumerate(((a_hi, b_hi), (a_hi, b_lo), (a_lo, b_hi))):
                        last = pe.matmul(dst, u(k), v(k), start=start and k == kts[0] and i == 0,
                                         stop=stop and k == kts[-1] and i == 2)
                return last

            pe.wait_ge(s_cst, 16)
            pe.wait_ge(s_vec, 16 * 6)
            pe.transpose(bank(6)[:, 0:N_VEC], vec_rows[:], ident[0:N_VEC, 0:N_VEC]).then_inc(s_vecT, 1)
            pe.wait_ge(s_tap, 16)
            for t in range(CT):
                last = pe.transpose(bank(7)[:, t * KC:(t + 1) * KC], tap_rows[:, t * P:(t + 1) * P], ident[0:KC, 0:KC])
            last.then_inc(s_tapT, 1)

            for k in range(KT):
                if k == 0:
                    pe.wait_ge(s_xn, TT)
                if k >= 2:
                    pe.wait_ge(s_hfull, k - 1)
                for i in range(TT):
                    last = pe.transpose(pair[k % 2][:, i * P:(i + 1) * P], x_rows[:, i, k * P:(k + 1) * P], ident)
                last.then_inc(s_xT, 1)
                if k == 1:
                    pe.wait_ge(s_adastep, KT)
                    pe.wait_ge(s_cols, 1)
                    for j in range(16):
                        last = pe.matmul(bank(6)[:, j:j + 1], ada_acc[:, j * P:(j + 1) * P], ones[:, 0:1], start=True, stop=True)
                    last.then_inc(s_modp, 1)

            def mod_rows(half):
                pe.wait_ge(s_adastep, KT * (half + 2))
                for j in range(4):
                    m = 4 * half + j
                    if m >= 2:
                        pe.wait_ge(s_modfree, m - 1)
                    else:
                        pe.wait_ge(s_modc, 1)
                        pe.wait_ge(s_taps, 1)
                    pe.matmul(bank(6 + m % 2)[0:1, :], ones[:, 0:1], ada_acc[:, j * CW:(j + 1) * CW],
                              start=True, stop=True).then_inc(s_modp, 1)

            def tile_begin(m):
                if m >= 4:
                    pe.wait_ge(s_tfree, m - 3)
                if m % 8 == 0:
                    C = m // 8
                    pe.wait_ge(s_hi, C + 1)
                    pe.wait_ge(s_lo, C + 1)
                    pe.wait_ge(s_plo, C + 1)
                return bank(m % 4)

            def w(parts, C, n0=0, n1=CW):
                return lambda k: parts[C % 2][:, k, n0:n1]

            def rows_of(parts, i):
                return lambda k: parts[:, k, i * P:(i + 1) * P]

            pe.wait_ge(s_hlo, KT)
            pe.wait_ge(s_hhi, KT)
            for C in (A_CH, GT_CH):
                for t in range(CT):
                    for half in range(2):
                        m = C * 8 + t * 2 + half
                        dst = tile_begin(m)
                        tok = lambda parts: (lambda k: parts[:, k, half * CW:(half + 1) * CW])
                        product(dst, w(w_hi, C, t * P, t * P + P), w(w_lo, C, t * P, t * P + P), tok(op_hi), tok(op_lo),
                                range(KT), True, True).then_inc(s_tile, 1)
                mod_rows(C)

            def qk_transposes(j):
                pe.wait_ge(s_qn, j + 1)
                if j >= 2:
                    pe.wait_ge(s_qkev, j - 1)
                for g in range(4):
                    src = k_row[:, g * P:(g + 1) * P] if j < TT else q_tmp[:, g, (j - TT) * P:(j - TT + 1) * P]
                    last = pe.transpose(bank(4 + j % 2)[:, g * P:(g + 1) * P], src, ident)
                last.then_inc(s_qkT, 1)

            for C in (K_CH, V_CH, Q_CH):
                for i in range(TT):
                    m = C * 8 + i
                    dst = tile_begin(m)
                    product(dst, rows_of(op_hi, i), rows_of(op_lo, i), w(w_hi, C), w(w_lo, C), range(KT), True, True
                            ).then_inc(s_tile, 1)
                    if C == K_CH and i:
                        qk_transposes(i - 1)
                    if C == V_CH and i == 0:
                        qk_transposes(TT - 1)
                    if C == Q_CH and i:
                        qk_transposes(TT + i - 1)
            qk_transposes(2 * TT - 1)
            pe.wait_ge(s_qkev, 2 * TT)

            units = [(j, h) for j in range(TT) for h in range(NH)]

            def scores(u):
                j, h = units[u]
                nk = min(j, 4) + 1
                if u >= 2:
                    pe.wait_ge(s_Sfree, u - 1)
                else:
                    pe.wait_ge(s_tfree, 8 * 5)
                lo, g = h % 2 * HD, h // 2
                for n0 in range(0, nk * P, CW):
                    n1 = min(n0 + CW, nk * P)
                    last = pe.matmul(pair[u % 2][:, n0:n1], qT[lo:lo + HD, g, j * P:(j + 1) * P],
                                     kT[lo:lo + HD, g, (j + 1 - nk) * P + n0:(j + 1 - nk) * P + n1], start=True, stop=True)
                last.then_inc(s_S, 1)

            def turn_probs(u):
                nk = min(units[u][0], 4) + 1
                pe.wait_ge(s_exp, u + 1)
                if u >= 1:
                    pe.wait_ge(s_pTc, u)
                if units[u][1] == 2 and units[u][0]:
                    pe.wait_ge(s_yhi, units[u][0])
                    pe.wait_ge(s_ylo, units[u][0])
                for k in range(nk):
                    last = pe.transpose(pair[2][:, k * P:(k + 1) * P], s_sb[u % 2][:, k * P:(k + 1) * P], ident)
                last.then_inc(s_PT, 1)

            def weigh_values(u):
                j, h = units[u]
                nk = min(j, 4) + 1
                pe.wait_ge(s_pTc, u + 1)
                if h == 0 and j >= 2:
                    pe.wait_ge(s_y, j - 1)
                for k in range(nk):
                    last = pe.matmul(bank(6 + j % 2)[:, h * HD:(h + 1) * HD], p_T[u % 2][:, k * P:(k + 1) * P],
                                     v_rows[:, j + 1 - nk + k, h * HD:(h + 1) * HD], start=(k == 0), stop=(k == nk - 1))
                last.then_inc(s_PV, 1)

            def turn_outputs(j):
                pe.wait_ge(s_y, j + 1)
                pe.wait_ge(s_pTc, min(NH * (j + 1) + 2, len(units)))
                for g in range(4):
                    last = pe.transpose(pair[2][:, g * P:(g + 1) * P], y_row[:, g * P:(g + 1) * P], ident)
                last.then_inc(s_yT, 1)

            for u in range(len(units) + 2):
                if u < len(units):
                    scores(u)
                if 1 <= u <= len(units):
                    turn_probs(u - 1)
                if u >= 2:
                    weigh_values(u - 2)
                    if u >= 10 and (u - 2) % NH == 0:
                        turn_outputs((u - 2) // NH - 1)
            turn_outputs(TT - 1)

            pe.wait_ge(s_dve, CT * KC)
            pe.wait_ge(s_Sfree, len(units))
            for half in range(2):
                for t in range(CT):
                    last = pe.matmul(bank(half), ones, uT[:, t, KC - 1 + half * CW:KC - 1 + (half + 1) * CW],
                                     start=(t == 0), stop=(t == CT - 1))
                last.then_inc(s_lnsum, 1)
            for t in range(CT):
                pe.wait_ge(s_lnsq, t + 1)
                for half in range(2):
                    last = pe.matmul(bank(2 + half), ones, ln_sq(t)[:, half * CW:(half + 1) * CW],
                                     start=(t == 0), stop=(t == CT - 1))
                last.then_inc(s_lnvar, 1)

            pe.wait_ge(s_lnhi, CT)
            pe.wait_ge(s_lnlo, CT)
            pe.wait_ge(s_yhi, TT)
            pe.wait_ge(s_ylo, TT)

            def h2_turn(i):
                pe.wait_ge(s_h2, i + 1)
                if i >= 1:
                    pe.wait_ge(s_h2Tc, i)
                for k in range(KT):
                    last = pe.transpose(pair[2][:, k * P:(k + 1) * P], h2r[:, k, i * P:(i + 1) * P], ident)
                last.then_inc(s_h2T, 1)

            def router(i):
                pe.wait_ge(s_h2Tc, i + 1)
                pe.wait_ge(s_rows, 16 * 7)
                for k in range(KT):
                    last = pe.matmul(bank(6)[:, i * E:(i + 1) * E], h2T[:, k, i * P:(i + 1) * P], rw[:, k, :],
                                     start=(k == 0), stop=(k == KT - 1))
                last.then_inc(s_lg, 1)

            for C in (O_CH, O_CH + 1):
                for i in range(TT):
                    m = C * 8 + i
                    dst = tile_begin(m)
                    product(dst, rows_of(op_hi, i), rows_of(op_lo, i), w(w_hi, C), w(w_lo, C), range(KT), True, True
                            ).then_inc(s_tile, 1)
                    if C > O_CH and i >= 1:
                        h2_turn(i - 1)
                    if C > O_CH and i >= 2:
                        router(i - 2)
            h2_turn(TT - 1)
            router(TT - 2)
            router(TT - 1)

            pe.wait_ge(s_c2, 16)
            pe.wait_ge(s_mk, 1)
            pe.matmul(bank(0)[:, 0:TT * E], tri, mask[:].rearrange("p i e -> p (i e)"), start=True, stop=True).then_inc(s_rk, 1)
            pe.matmul(bank(1)[:, 0:TT * E], ones, mask[:].rearrange("p i e -> p (i e)"), start=True, stop=True).then_inc(s_rk, 1)
            for i in range(TT):
                last = pe.matmul(bank(2)[0:CAND, 0:1], mask2[:, i, :], ones[:, 0:1], start=(i == 0), stop=(i == TT - 1))
            last.then_inc(s_cn, 1)
            pe.wait_ge(s_cv, 1)
            pe.matmul(bank(3)[0:CAND, 0:2], stri, cand[:, 0:2], start=True, stop=True).then_inc(s_pf, 1)
            pe.wait_ge(s_sl, 1)
            for r, col in enumerate((5, 1, 3, 4)):
                pe.matmul(bank(4)[0:1, r * TABW:(r + 1) * TABW], cand[:, col:col + 1], sel[:], start=True, stop=True)
            pe.matmul(bank(4)[0:1, 4 * TABW:4 * TABW + 2], ones[0:CAND, 0:1], cand[:, 0:2], start=True, stop=True).then_inc(m_done, 1)
            pe.matmul(bank(5)[:, 0:TABW], base_rep[:], sel[:], start=True, stop=True).then_inc(s_tb, 1)


            def find(b, ix, first, B=None, n=None):
                pe.wait_ge(oh_ok, ix + 1)
                if not first or b:
                    pe.wait_ge(idx_ok, ix)
                if not first:
                    pe.wait_ge(x_h, B * 2 + n * 2)
                    pe.wait_ge(x_l, B * 2 + n * 2)
                for t in range(TT):
                    last = pe.matmul(bank(7)[:, 4 * b:4 * b + 4], onehot[:, t, :], rhs[:, t, :], start=(t == 0), stop=(t == TT - 1))
                last.then_inc(i_ps, 1)

            def turn_x(b, ix, before, first, found):
                pe.wait_ge(g_in, ix * 16 + 16)
                pe.wait_ge(idx_ok, found)
                for half in range(2):
                    if not first or b:
                        free = before * 2 + (half + 1 if b else 0)
                        pe.wait_ge(x_h, free)
                        pe.wait_ge(x_l, free)
                    for k in range(4):
                        col = (half * 4 + k) * P
                        last = pe.transpose(bank(6 + half)[:, k * P:(k + 1) * P], xg[b][:, col:col + P], ident)
                    last.then_inc(x_ps, 1)

            pe.wait_ge(s_tab, 1)
            passes = pe.value_load(tab[0:1, 4 * TABW:4 * TABW + 1], min_val=1, max_val=TABW - 2)
            n0 = pe.value_load(tab[0:1, TABW + 1:TABW + 2], min_val=1, max_val=MAXB)
            for b in range(MAXB):
                def first_block():
                    find(b, b, True)
                if b:
                    with pe.If(n0 > b):
                        first_block()
                else:
                    first_block()
            for b in range(MAXB):
                if b:
                    with pe.If(n0 > b):
                        turn_x(b, b, max(b - 1, 0), True, n0 + 0)
                else:
                    turn_x(b, b, max(b - 1, 0), True, n0 + 0)

            with pe.Fori(0, passes) as p:
                n = pe.value_load(tab[0:1, bass.ds(p + (TABW + 1), 1)], min_val=1, max_val=MAXB)
                n2 = pe.value_load(tab[0:1, bass.ds(p + (TABW + 2), 1)], min_val=0, max_val=MAXB)
                n_p = pe.value_load(tab[0:1, bass.ds(p + TABW, 1)], min_val=0, max_val=MAXB)
                B = pe.value_load(tab[0:1, bass.ds(p + (2 * TABW + 1), 1)], min_val=0, max_val=64)
                w0 = pe.value_load(tab[0:1, bass.ds(p + 3 * TABW, 1)], min_val=0, max_val=512)

                def turn_act(c_, b):
                    it = B * 4 + n * c_ + b
                    pe.wait_ge(act_ok, it + 1)
                    pe.wait_ge(aT_h, it + 1)
                    pe.wait_ge(aT_l, it + 1)
                    for k in range(2):
                        last = pe.transpose(bank(5)[:, k * P:(k + 1) * P], act_r[b][:, k * P:(k + 1) * P], ident)
                    last.then_inc(aT_ps, 1)

                def block_product(c_, b):
                    par = (X_CH + c_) % 2
                    dst = bank(u_bank[b][c_ % 2])
                    if b == 0:
                        if c_ < 2:
                            pe.wait_ge(m_free, w0 + n_p * c_ + 2)
                        else:
                            pe.wait_ge(m_free, B * NPC + n * (c_ - 2) + 3)
                    elif c_ == 0:
                        pe.wait_ge(m_free, B * NPC + 2)
                    else:
                        pe.wait_ge(m_free, B * NPC + n * (c_ - 1) + (b + 3))
                    w_of = lambda parts: (lambda k: parts[par][:, k, :])
                    if c_ < 4:
                        if c_ == 0:
                            pe.wait_ge(x_h, B * 2 + (2 * b + 2))
                            pe.wait_ge(x_l, B * 2 + (2 * b + 2))
                        x_of = lambda parts: (lambda k: parts[b][:, k, :])
                        product(dst, x_of(xT_hi), x_of(xT_lo), w_of(w_hi), w_of(w_lo), range(KT), True, True).then_inc(m_done, 1)
                        if c_:
                            turn_act(c_ - 1, b)
                    else:
                        a_of = lambda parts: (lambda k: parts[b][:, k, :])
                        args = (a_of(aT_hi), a_of(aT_lo), w_of(w_hi), w_of(w_lo))
                        if c_ == 4:
                            pe.wait_ge(aT_h, B * 4 + n * 2 + (b + 2))
                            pe.wait_ge(aT_l, B * 4 + n * 2 + (b + 2))
                            product(dst, *args, range(6), True, False)
                            turn_act(3, b)
                            pe.wait_ge(aT_h, B * 4 + n * 3 + (b + 2))
                            pe.wait_ge(aT_l, B * 4 + n * 3 + (b + 2))
                            product(dst, *args, range(6, KT), False, True).then_inc(m_done, 1)
                        else:
                            product(dst, *args, range(KT), True, True).then_inc(m_done, 1)

                for c_ in range(NPC):
                    pe.wait_ge(s_hi, p * NPC + (X_CH + c_ + 1))
                    pe.wait_ge(s_lo, p * NPC + (X_CH + c_ + 1))
                    pe.wait_ge(s_plo, p * NPC + (X_CH + c_ + 1))
                    for b in range(MAXB):
                        if c_ == NPC - 1:
                            with pe.If(n2 > b):
                                turn_x(b, B + n + b, B + n + max(b - 1, 0), False, B + n + n2)
                        if b:
                            with pe.If(n > b):
                                block_product(c_, b)
                        else:
                            block_product(c_, b)
                    if 1 <= c_ <= 4:
                        with pe.If(n2 > c_ - 1):
                            find(c_ - 1, B + n + (c_ - 1), False, B, n)

        @block.scalar
        def _(act):
            act.wait_ge(s_cols, 1)
            act.activation(c_act[:, 0:8], cols[:, V_C:V_C + 8], ACT.Sigmoid).then_inc(s_csig, 1)
            for i in range(TT):
                act.wait_ge(s_x[i // 4], 16)
                act.activation(pair[2][:], x_rows[:, i, :], ACT.Square, accum_out=stat[:, i:i + 1])
                act.drain()
            act.drain()
            act.activation(stat[:, 8:16], stat[:, 0:8], ACT.Sqrt, bias=eps_col, scale=1.0 / D).then_inc(s_xroot, 1)
            write_hi(act, 0, 0, 16)

            for k in range(KT):
                act.wait_ge(s_xT, k + 1)
                act.wait_ge(s_modc, 1)
                if k >= 2:
                    act.wait_ge(s_hlo, k - 1)
                act.activation(h_full[k % 2][:], pair[k % 2][:], ACT.Identity, bias=mod_col[:, k:k + 1],
                               scale=mod_col[:, 8 + k:9 + k]).then_inc(s_hfull, 1)
                act.wait_ge(s_hfull, k + 1)
                act.activation(op_hi[:, k, :], h_full[k % 2][:], ACT.Copy).then_inc(s_hhi, 1)

            def split(C):
                before_trunk_split(act, C)
                write_hi(act, C % 2, 0, 16 * (C + 1))

            split(1)
            split(2)
            for j in range(8):
                m = GT_CH * 8 + j
                act.wait_ge(s_tile, m + 1)
                if j >= 2:
                    act.wait_ge(s_uz, j - 1)
                act.activation(sig_t[j % 2][:], bank(m % 4), ACT.Sigmoid).then_inc(s_gsig, 1)

            def turned(j):
                act.wait_ge(s_qkT, j + 1)
                i = j % TT
                dst = kT[:, 0:4, i * P:(i + 1) * P] if j < TT else qT[:, 0:4, i * P:(i + 1) * P]
                act.activation(dst, bank(4 + j % 2).rearrange("p (g n) -> p g n", n=P), ACT.Copy).then_inc(s_qkev, 1)

            def roots(j, m):
                act.wait_ge(s_tile, m + 1)
                if j < TT:
                    if j:
                        act.wait_ge(s_qss, j)
                    dst = k_sq[:].rearrange("p (g n) -> p g n", n=P)
                else:
                    dst = q_tmp[:, 4:8, (j - TT) * P:(j - TT + 1) * P]
                act.activation(dst, bank(m % 4).rearrange("p (g n) -> p g n", n=P), ACT.Square).then_inc(s_qsq, 1)
                act.wait_ge(s_qss, j + 1)
                if j < TT:
                    act.activation(sq_root[:], sq_sum[:], ACT.Sqrt, bias=eps_col, scale=1.0 / HD).then_inc(s_qroot, 1)
                else:
                    act.activation(sq_root[:], sq_sum[:], ACT.Sqrt, bias=eps64_col, scale=1.0).then_inc(s_qroot, 1)

            split(3)
            for i in range(TT):
                roots(i, K_CH * 8 + i)
                if i:
                    turned(i - 1)
            split(4)
            turned(TT - 1)
            split(5)
            for i in range(TT):
                roots(TT + i, Q_CH * 8 + i)
                if i:
                    turned(TT + i - 1)
            turned(2 * TT - 1)

            def copy_probs(u):
                nk = min(u // NH, 4) + 1
                act.wait_ge(s_PT, u + 1)
                if u >= 2:
                    act.wait_ge(s_PV, u - 1)
                act.activation(p_T[u % 2][:, 0:nk * P], pair[2][:, 0:nk * P], ACT.Copy).then_inc(s_pTc, 1)

            def copy_outputs(j):
                act.wait_ge(s_yT, j + 1)
                act.activation(op_hi[:, 4:8, j * P:(j + 1) * P], pair[2][:, 0:CW].rearrange("p (g n) -> p g n", n=P),
                               ACT.Copy).then_inc(s_yhi, 1)

            for u in range(NH * TT):
                if u:
                    copy_probs(u - 1)
                j, h = u // NH, u % NH
                nk = min(j, 4) + 1
                act.wait_ge(s_nmx, u + 1)
                act.activation(s_sb[u % 2][:, 0:nk * P], s_sb[u % 2][:, 0:nk * P], ACT.Exp,
                               bias=mx[:, u % 2 * 4 + 2:u % 2 * 4 + 3], accum_out=rsum[:, j % 2 * 8 + h:j % 2 * 8 + h + 1]
                               ).then_inc(s_exp, 1)
                if j and h == 2:
                    copy_outputs(j - 1)
            copy_probs(NH * TT - 1)
            copy_outputs(TT - 1)

            for t in range(CT):
                act.wait_ge(s_lnc, t + 1)
                if t == 0:
                    act.wait_ge(s_PV, NH * TT)
                if t >= 2:
                    act.wait_ge(s_lnvar, t - 1)
                act.activation(ln_sq(t)[:], uT[:, t, KC - 1:], ACT.Square).then_inc(s_lnsq, 1)
            act.wait_ge(s_lnvar, CT)
            act.activation(ln_r[:], pair[1][:], ACT.Sqrt, bias=eps_col, scale=1.0 / 512).then_inc(s_lnroot, 1)

            def conv_hi(t):
                act.wait_ge(s_lny, t + 1)
                act.activation(op_hi[:, t, :], uT[:, t, KC - 1:], ACT.Copy).then_inc(s_lnhi, 1)

            for t in range(CT):
                act.wait_ge(s_lnz, t + 1)
                if t >= 2:
                    act.wait_ge(s_lny, t - 1)
                act.activation(ln_sig(t)[:], uT[:, t, KC - 1:], ACT.Sigmoid, bias=cols[:, V_LB + t:V_LB + t + 1]).then_inc(s_lnsig, 1)
                if t:
                    conv_hi(t - 1)
            conv_hi(CT - 1)

            split(6)

            def turned_h2(i):
                act.wait_ge(s_h2T, i + 1)
                act.activation(h2T[:, :, i * P:(i + 1) * P], pair[2][:].rearrange("p (k n) -> p k n", n=P), ACT.Copy).then_inc(s_h2Tc, 1)

            for i in range(TT):
                act.wait_ge(s_x2, i + 1)
                act.activation(h2T[:, :, i * P:(i + 1) * P], x2[:, i, :].rearrange("p (k n) -> p k n", n=P), ACT.Square,
                               accum_out=stat[:, i:i + 1])
                act.drain()
                act.activation(stat[:, 8 + i:9 + i], stat[:, i:i + 1], ACT.Sqrt, bias=eps_col, scale=1.0 / D).then_inc(s_x2root, 1)
                if i:
                    turned_h2(i - 1)
            turned_h2(TT - 1)

            act.wait_ge(s_nm, 1)
            act.activation(gex[:], gex[:], ACT.Exp).then_inc(s_gex, 1)

            act.wait_ge(s_tab, 1)
            act.activation(sg[:, 0:1], pad_id, ACT.Copy).then_inc(aT_h, 1)
            passes = act.value_load(tab[0:1, 4 * TABW:4 * TABW + 1], min_val=1, max_val=TABW - 2)
            n0 = act.value_load(tab[0:1, TABW + 1:TABW + 2], min_val=1, max_val=MAXB)
            write_hi(act, X_CH % 2, X_CH % 2, 32)

            def x_hi(b, ix):
                for half in range(2):
                    act.wait_ge(x_ps, ix * 2 + (half + 1))
                    act.activation(xT_hi[b][:, 4 * half:4 * half + 4, :], bank(6 + half).rearrange("p (k n) -> p k n", n=P),
                                   ACT.Copy).then_inc(x_h, 1)

            x_hi(0, 0)
            for b in range(1, MAXB):
                with act.If(n0 > b):
                    x_hi(b, b)
            with act.Fori(0, passes) as p:
                n = act.value_load(tab[0:1, bass.ds(p + (TABW + 1), 1)], min_val=1, max_val=MAXB)
                n2 = act.value_load(tab[0:1, bass.ds(p + (TABW + 2), 1)], min_val=0, max_val=MAXB)
                B = act.value_load(tab[0:1, bass.ds(p + (2 * TABW + 1), 1)], min_val=0, max_val=64)

                def next_hi(c_):
                    d = (c_ + 1) % NPC
                    more = 0 if c_ < NPC - 1 else 1
                    act.wait_ge(m_done, B * NPC + n * c_ + 1)
                    landed = p * 80 + (80 * more + {0: 32, 2: 64, 4: 80, 1: 112 + 32, 3: 112 + 64, 5: 112 + 80}[d])
                    write_hi(act, (X_CH + d) % 2, (X_CH + d) % 2, landed)

                def block_step(c_, b):
                    if 1 <= c_ <= 4:
                        act.wait_ge(aT_ps, B * 4 + n * (c_ - 1) + (b + 1))
                        act.activation(aT_hi[b][:, 2 * (c_ - 1):2 * c_, :], bank(5)[:, 0:2 * P].rearrange("p (k n) -> p k n", n=P),
                                       ACT.Copy).then_inc(aT_h, 1)
                    if c_ < 4:
                        act.wait_ge(glu_ok, B * 4 + n * c_ + (b + 1))
                        act.activation(sg[:], ut[:, 0:SQ], ACT.Sigmoid, scale=ALPHA).then_inc(sig_ok, 1)

                for c_ in range(NPC):
                    if c_ < NPC - 1:
                        next_hi(c_)
                    else:
                        with act.If(n2 > 0):
                            next_hi(c_)
                    for b in range(MAXB):
                        if c_ == NPC - 1:
                            with act.If(n2 > b):
                                x_hi(b, B + n + b)
                        elif b:
                            with act.If(n > b):
                                block_step(c_, b)
                        else:
                            block_step(c_, b)

        @block.vector
        def _(ve):
            def lo_part(C):
                before_trunk_split(ve, C)
                write_lo(ve, C % 2, 0, C + 1, slice(0, V_KT), s_lo)

            ve.wait_ge(s_vecT, 1)
            ve.tensor_copy(cols[:], bank(6)[:, 0:N_VEC]).then_inc(s_cols, 1)
            ve.wait_ge(s_tapT, 1)
            ve.tensor_copy(taps[:].rearrange("p t k -> p (t k)"), bank(7)[:, 0:CT * KC]).then_inc(s_taps, 1)
            ve.wait_ge(s_csig, 1)
            ve.wait_ge(s_cols, 1)
            ve.tensor_tensor(c_act[:, 8:16], cols[:, V_C:V_C + 8], c_act[:, 0:8], ALU.mult)
            ve.drain()

            def ada_step(n):
                k = n % KT
                ve.wait_ge(s_ada[n % 2], 16 * (n // 2 + 1))
                if k == 0:
                    if n:
                        ve.wait_ge(s_modp, 1 if n == KT else 5)
                    ve.tensor_scalar(ada_acc[:], ada_t[n % 2][:], c_act[:, 8:9], None, ALU.mult).then_inc(s_adastep, 1)
                else:
                    ve.wait_ge(s_adastep, n)
                    ve.scalar_tensor_tensor(ada_acc[:], ada_t[n % 2][:], c_act[:, 8 + k:9 + k], ada_acc[:],
                                            ALU.mult, ALU.add).then_inc(s_adastep, 1)

            for n in range(4):
                ada_step(n)
            ve.wait_ge(s_relrow, 16)
            ve.tensor_copy(mx[0:NH, 0:1], rel_rows[:, 256:257])
            ve.memset(rel_rows[:, 257:384], 0.0)
            ve.drain()
            ve.tensor_scalar(rel_rows[:, 0:257], rel_rows[:, 0:257], mx[0:NH, 0:1], None, ALU.subtract).then_inc(s_rel, 1)
            ve.wait_ge(s_xroot, 1)
            ve.reciprocal(stat[:, 0:8], stat[:, 8:16])
            ve.drain()
            for i in range(TT):
                ve.tensor_scalar(x_rows[:, i, :], x_rows[:, i, :], stat[:, i:i + 1], None, ALU.mult).then_inc(s_xn, 1)
            for n in range(4, 8):
                ada_step(n)
            lo_part(0)
            ve.wait_ge(s_modp, 1)
            ve.tensor_tensor(mod_col[:], bank(6)[:, 0:16], cols[:, V_ADA:V_ADA + 16], ALU.add)
            ve.drain()
            ve.scalar_tensor_tensor(mod_col[:, 8:16], mod_col[:, 8:16], 1.0, cols[:, V_G1:V_G1 + 8], ALU.add, ALU.mult).then_inc(s_modc, 1)
            for k in range(KT):
                ve.wait_ge(s_hhi, k + 1)
                ve.tensor_tensor(op_lo[:, k, :], h_full[k % 2][:], op_hi[:, k, :].bitcast(F32), ALU.subtract).then_inc(s_hlo, 1)
            ve.wait_ge(s_hlo, KT)
            ve.memset(uT[:, :, 0:KC - 1], 0.0)

            def mod_values(half):
                ve.wait_ge(s_adab, 16 * (half + 1))
                for j in range(4):
                    m = 4 * half + j
                    ve.wait_ge(s_modp, m + 2)
                    row = mod_row[0:1, j * CW:(j + 1) * CW]
                    ve.tensor_tensor(row, row, bank(6 + m % 2)[0:1, :], ALU.add).then_inc(s_modfree, 1)
                ve.wait_ge(s_modfree, 4 * half + 4)
                ve.sem_inc(s_modr, 1)

            for m in range(8):
                ve.wait_ge(s_tile, m + 1)
                t, half = m // 2, m % 2
                ve.tensor_copy(uT[:, t, KC - 1 + half * CW:KC - 1 + (half + 1) * CW], bank(m % 4)).then_inc(s_tfree, 1)
                if m == 1:
                    lo_part(1)
                if m >= 2:
                    ada_step(KT + m - 2)
            ada_step(2 * KT - 2)
            ada_step(2 * KT - 1)
            mod_values(0)
            for j in range(8):
                m = GT_CH * 8 + j
                t, half = j // 2, j % 2
                ve.wait_ge(s_gsig, j + 1)
                u = uT[:, t, KC - 1 + half * CW:KC - 1 + (half + 1) * CW]
                ve.wait_ge(s_tfree, t * 2 + half + 1)
                ve.tensor_tensor(u, u, sig_t[j % 2][:], ALU.mult).then_inc(s_uz, 1)
                ve.wait_ge(s_uz, j + 1)
                ve.sem_inc(s_tfree, 1)
                if j == 1:
                    lo_part(2)
                ada_step(2 * KT + j)
            mod_values(1)

            conv_done = [0]

            def conv_steps(count):
                for _ in range(count):
                    s = conv_done[0]
                    if s == CT * KC:
                        return
                    ct, tap = s // KC, s % KC
                    src = uT[:, ct, tap:tap + T]
                    w_tap = taps[:, ct, tap:tap + 1]
                    if s:
                        ve.wait_ge(s_dve, s)
                    if tap == 0:
                        ve.tensor_scalar(acc[:], src, w_tap, cols[:, V_CB + ct:V_CB + ct + 1], ALU.mult, ALU.add).then_inc(s_dve, 1)
                    else:
                        dst = acc[:] if tap < KC - 1 else uT[:, ct, KC - 1:]
                        ve.scalar_tensor_tensor(dst, src, w_tap, acc[:], ALU.mult, ALU.add).then_inc(s_dve, 1)
                    conv_done[0] += 1

            ve.wait_ge(s_gain, 32)

            def normalise(j, m):
                ve.wait_ge(s_qsq, j + 1)
                cols_j = slice((j % TT) * P, (j % TT + 1) * P)
                sq = k_sq[:].rearrange("p (g h d) -> p g h d", h=2, d=HD) if j < TT else q_tmp[:, 4:8, cols_j].rearrange("p g (h d) -> p g h d", d=HD)
                ve.tensor_reduce(sq_sum[:].rearrange("p (g h) -> p g h", h=2), sq, AX_X, ALU.add).then_inc(s_qss, 1)
                conv_steps(1)
                ve.wait_ge(s_qroot, j + 1)
                ve.reciprocal(sq_inv[:], sq_root[:])
                if 1 <= j < TT:
                    ve.wait_ge(s_qkT, j)
                ve.drain()
                dst = k_row[:].rearrange("p (g h d) -> p g h d", h=2, d=HD) if j < TT else q_tmp[:, 0:4, cols_j].rearrange("p g (h d) -> p g h d", d=HD)
                ve.tensor_tensor(dst, bank(m % 4).rearrange("p (g h d) -> p g h d", h=2, d=HD),
                                 view(sq_inv[:], [[2, 4], [1, 2], [0, HD]]), ALU.mult).then_inc(s_tfree, 1)
                ve.wait_ge(s_tfree, m + 1)
                ve.tensor_tensor(dst, dst, view(gains[:, 1 if j < TT else 0, :], [[0, 4], [0, 2], [1, HD]]), ALU.mult).then_inc(s_qn, 1)

            for i in range(TT):
                if i == 0:
                    ve.wait_ge(s_modst, 32)
                normalise(i, K_CH * 8 + i)
                conv_steps(2)
                if i == 1:
                    lo_part(3)
            for i in range(TT):
                if i == 0:
                    ve.wait_ge(s_qkT, TT)
                ve.wait_ge(s_tile, V_CH * 8 + i + 1)
                ve.tensor_copy(v_rows[:, i, :], bank((V_CH * 8 + i) % 4)).then_inc(s_tfree, 1)
                if i == 1:
                    lo_part(4)
                conv_steps(3)
            for i in range(TT):
                normalise(TT + i, Q_CH * 8 + i)
                if i == 1:
                    lo_part(5)
                conv_steps(2)

            ve.wait_ge(s_mask, 16)
            ve.wait_ge(s_relld, 16 * NH)
            ve.wait_ge(s_qn, 2 * TT)
            ve.tensor_tensor(near_bias[:, :, 0:64], near_bias[:, :, 0:64], view(masks[:], [[0, NH], [1, 64]], 3 * P), ALU.add)
            ve.drain()

            def attention_rows(j):
                ve.wait_ge(s_PV, NH * (j + 1))
                ve.reciprocal(r_inv[:], rsum[:, j % 2 * 8:j % 2 * 8 + 8])
                if j:
                    ve.wait_ge(s_yT, j)
                ve.drain()
                ve.tensor_tensor(y_row[:].rearrange("p (h d) -> p h d", d=HD), bank(6 + j % 2).rearrange("p (h d) -> p h d", d=HD),
                                 view(r_inv[:], [[1, NH], [0, HD]]), ALU.mult).then_inc(s_y, 1)

            def attention_lo(j):
                ve.wait_ge(s_yT, j + 1)
                ve.wait_ge(s_yhi, j + 1)
                cols_j = slice(j * P, (j + 1) * P)
                ve.tensor_tensor(op_lo[:, 4:8, cols_j], pair[2][:, 0:CW].rearrange("p (g n) -> p g n", n=P),
                                 op_hi[:, 4:8, cols_j].bitcast(F32), ALU.subtract).then_inc(s_ylo, 1)

            for u in range(NH * TT):
                j, h = u // NH, u % NH
                nk = min(j, 4) + 1
                nf = max(nk - 2, 0)
                ve.wait_ge(s_S, u + 1)
                if u >= 2:
                    ve.wait_ge(s_PT, u - 1)
                a, near = u % 2 * 4, (nk - nf) * P
                if nf:
                    ve.tensor_tensor_reduce(s_sb[u % 2][:, 0:nf * P], pair[u % 2][:, 0:nf * P], masks[:, (3 - nf) * P:3 * P],
                                            1.0, NEG, ALU.add, ALU.max, mx[:, a:a + 1])
                ve.tensor_tensor_reduce(s_sb[u % 2][:, nf * P:nk * P], pair[u % 2][:, nf * P:nk * P],
                                        view(near_bias[:, h, :], [[-1, near]], near - 1), 1.0, NEG, ALU.add, ALU.max,
                                        mx[:, a + 1:a + 2]).then_inc(s_Sfree, 1)
                ve.wait_ge(s_Sfree, u + 1)
                if nf:
                    ve.tensor_scalar(mx[:, a + 2:a + 3], mx[:, a:a + 1], mx[:, a + 1:a + 2], -1.0, ALU.max, ALU.mult).then_inc(s_nmx, 1)
                else:
                    ve.tensor_scalar(mx[:, a + 2:a + 3], mx[:, a + 1:a + 2], -1.0, None, ALU.mult).then_inc(s_nmx, 1)
                conv_steps(1)
                if j and h == 1:
                    attention_rows(j - 1)
                if j and h == 2:
                    attention_lo(j - 1)
            attention_rows(TT - 1)
            attention_lo(TT - 1)

            ve.wait_ge(s_lnsum, 2)
            for t in range(CT):
                y = uT[:, t, KC - 1:]
                ve.scalar_tensor_tensor(y, pair[0][:], -1.0 / 512, y, ALU.mult, ALU.add).then_inc(s_lnc, 1)
            ve.wait_ge(s_lnroot, 1)
            ve.reciprocal(ln_r[:], ln_r[:])
            ve.drain()

            def conv_y(t):
                y = uT[:, t, KC - 1:]
                ve.wait_ge(s_lnsig, t + 1)
                ve.scalar_tensor_tensor(y, y, cols[:, V_LB + t:V_LB + t + 1], ln_sig(t)[:], ALU.add, ALU.mult).then_inc(s_lny, 1)

            def conv_lo(t):
                ve.wait_ge(s_lnhi, t + 1)
                ve.tensor_tensor(op_lo[:, t, :], uT[:, t, KC - 1:], op_hi[:, t, :].bitcast(F32), ALU.subtract).then_inc(s_lnlo, 1)

            for t in range(CT):
                y = uT[:, t, KC - 1:]
                ve.wait_ge(s_lnsq, t + 1)
                ve.scalar_tensor_tensor(y, y, cols[:, V_LG + t:V_LG + t + 1], ln_r[:], ALU.mult, ALU.mult).then_inc(s_lnz, 1)
                if t >= 1:
                    conv_y(t - 1)
                if t >= 2:
                    conv_lo(t - 2)
            conv_y(CT - 1)
            conv_lo(CT - 2)
            conv_lo(CT - 1)

            ve.wait_ge(s_rows, 16 * 7)
            ve.wait_ge(s_x2ld, 16)
            ve.scalar_tensor_tensor(a2_row[:], a2_row[:], 1.0, n2_row[:], ALU.add, ALU.mult)
            ve.drain()

            def add_tile(C, i):
                m, n0_ = C * 8 + i, (C - O_CH) * CW
                ve.wait_ge(s_tile, m + 1)
                ve.tensor_tensor(t_row[i % 2][:], bank(m % 4), g1_row[:, n0_:n0_ + CW], ALU.mult).then_inc(s_tfree, 1)
                ve.wait_ge(s_tfree, m + 1)
                half = x2[:, i, n0_:n0_ + CW]
                return ve.tensor_tensor(half, half, t_row[i % 2][:], ALU.add)

            def rows_h2(i):
                ve.wait_ge(s_x2root, i + 1)
                ve.reciprocal(stat[:, i:i + 1], stat[:, 8 + i:9 + i])
                ve.drain()
                h = h2r[:, :, i * P:(i + 1) * P]
                cut = lambda ap: ap.rearrange("p (k n) -> p k n", n=P)
                ve.scalar_tensor_tensor(h, cut(x2[:, i, :]), stat[:, i:i + 1], cut(a2_row[:]), ALU.mult, ALU.mult)
                ve.drain()
                ve.tensor_tensor(h, h, cut(sh2_row[:]), ALU.add).then_inc(s_h2, 1)

            for i in range(TT):
                add_tile(O_CH, i)
                if i == 1:
                    lo_part(6)
            for i in range(TT):
                add_tile(O_CH + 1, i).then_inc(s_x2, 1)
                if i:
                    rows_h2(i - 1)
            rows_h2(TT - 1)

            ve.wait_ge(s_lg, TT)
            ve.tensor_tensor(lgt[:], bank(6)[:, 0:TT * E].rearrange("p (i e) -> p i e", e=E), view(rb_row[:], [[0, TT], [1, E]]), ALU.add)
            ve.drain()
            for i in range(TT):
                ve.max(top[:, i, :], lgt[:, i, :])
            ve.drain()
            for i in range(TT):
                ve.max_index(top_i[:, i, :], top[:, i, :], lgt[:, i, :])
            ve.drain()
            ve.wait_ge(s_h2st, 16 * TT)
            ve.tensor_tensor(gex[:], top[:, :, 0:TOPK], view(top[:], [[8, TT], [0, TOPK]]), ALU.subtract).then_inc(s_nm, 1)
            ve.tensor_copy(top_f[:], top_i[:])
            ve.wait_ge(s_gex, 1)
            ve.tensor_reduce(gsum[:], gex[:], AX_X, ALU.add)
            ve.drain()
            ve.reciprocal(ginv[:], gsum[:])
            ve.drain()
            ve.tensor_tensor(gex[:], gex[:], view(ginv[:], [[1, TT], [0, TOPK]]), ALU.mult)
            ve.wait_ge(s_iota, 16)
            ve.drain()
            per_tile = lambda t, r, step: view(t[:], [[step, TT], [0, E]], r)
            for r in range(TOPK):
                ve.tensor_tensor(hot[:], view(iota[:], [[0, TT], [1, E]]), per_tile(top_f, r, 8), ALU.is_equal)
                ve.drain()
                ve.tensor_tensor(hotg[:] if r else gate_te[:], hot[:], per_tile(gex, r, TOPK), ALU.mult)
                if r:
                    ve.tensor_tensor(mask[:], mask[:], hot[:], ALU.add)
                    ve.drain()
                    ve.tensor_tensor(gate_te[:], gate_te[:], hotg[:], ALU.add)
                else:
                    ve.tensor_copy(mask[:], hot[:])
                ve.drain()
            ve.tensor_copy(mask2[:].rearrange("p i (e s) -> p i e s", s=SPLITS),
                           view(mask[:], [[E, TT], [1, E], [0, SPLITS]])).then_inc(s_mk, 1)
            ve.tensor_copy(gate_et[:], view(gate_te[:], [[1, E], [E, TT]]))

            ve.wait_ge(s_c2, 16)
            ve.wait_ge(s_cn, 1)
            ve.tensor_copy(cand[:, 6:7], bank(2)[0:CAND, 0:1])
            ve.tensor_copy(cand[:, 5:6], cand_val[:, 0:1])
            ve.tensor_scalar(base_rep[:], ones[0:CAND, :], cand_val[:, 1:2], None, ALU.mult)
            ve.drain()
            ve.tensor_scalar(cmp[:], thr, cand[:, 6:7], None, ALU.is_lt)
            ve.drain()
            ve.tensor_reduce(cand[:, 1:2], cmp[:], AX_X, ALU.add)
            ve.tensor_copy(cand[:, 0:1], cmp[:, 0:1]).then_inc(s_cv, 1)
            ve.drain()
            ve.wait_ge(s_pf, 1)
            ve.tensor_copy(cand[:, 2:4], bank(3)[0:CAND, 0:2])
            ve.drain()
            ve.tensor_scalar(cand[:, 4:5], cand[:, 3:4], float(NPC), 1.0, ALU.mult, ALU.add)
            ve.tensor_scalar(sel[:], row_m1, cand[:, 2:3], cand[:, 0:1], ALU.is_equal, ALU.mult)
            ve.drain()
            ve.scalar_tensor_tensor(cand[:, 4:5], cand[:, 1:2], 4.0, cand[:, 4:5], ALU.mult, ALU.add).then_inc(s_sl, 1)

            ve.wait_ge(s_rk, 2)
            ve.memset(pre[:, 0, :], 0.0)
            for i in range(1, TT):
                ve.drain()
                ve.tensor_tensor(pre[:, i, :], pre[:, i - 1, :], bank(1)[:, (i - 1) * E:i * E], ALU.add)
            ve.drain()
            ve.tensor_tensor(rank[:], bank(0)[:, 0:TT * E].rearrange("p (i e) -> p i e", e=E), pre[:], ALU.add)
            ve.drain()
            ve.tensor_tensor(rank[:], rank[:], mask[:], ALU.mult)
            ve.drain()
            ve.tensor_scalar(pos_et[:], view(rank[:], [[1, E], [E, TT]]), -1.0, None, ALU.add)
            ve.tensor_copy(rhs[:, :, 0], tok_id)
            ve.tensor_copy(rhs[:, :, 3], ones[:, 0:TT])
            ve.wait_ge(s_tb, 1)
            ve.tensor_copy(pbase[:], bank(5)[:, 0:TABW]).then_inc(m_free, 1)
            ve.tensor_copy(g_idx[:], ones[:, 0:MAXB]).then_inc(m_free, 1)
            ve.tensor_copy(tab[0:1, 0:4 * TABW + 2], bank(4)[0:1, 0:4 * TABW + 2]).then_inc(aT_l, 1)
            ve.wait_ge(aT_l, 1)
            ve.wait_ge(m_free, 2)
            ve.sem_inc(s_tab, 1)

            def slots_of(e_, col):
                ve.tensor_scalar(posr[:], pos_et[:, bass.ds(e_, 1), :].rearrange("p e i -> p (e i)"), col, None, ALU.subtract)
                gates = gate_et[:, bass.ds(e_, 1), :].rearrange("p e i -> p (e i)")
                ve.tensor_copy(rhs[:, :, 1], gates)
                ve.drain()
                ve.tensor_tensor(rhs[:, :, 2], gates, rhs[:, :, 1].bitcast(F32), ALU.subtract)

            def mark(b, ix, first):
                if not first or b:
                    ve.wait_ge(i_ps, ix)
                ve.tensor_scalar(posb[:], posr[:], -float(P * b), None, ALU.add)
                ve.drain()
                ve.tensor_tensor(onehot[:], view(iota[:], [[0, TT], [1, P]]), view(posb[:], [[1, TT], [0, P]]), ALU.is_equal).then_inc(oh_ok, 1)

            def indices(b, ix):
                ve.wait_ge(i_ps, ix + 1)
                ve.tensor_copy(i_sb[:], bank(7)[:, 4 * b:4 * b + 4])
                ve.drain()
                ve.tensor_copy(g_idx[:, b:b + 1], i_sb[:, 0:1])
                ve.tensor_tensor(gt_nxt[:, b:b + 1], i_sb[:, 1:2], i_sb[:, 2:3], ALU.add)
                ve.scalar_tensor_tensor(s_tmp[:, 0:1], i_sb[:, 3:4], neg_pad, pad_id, ALU.mult, ALU.add)
                ve.drain()
                ve.tensor_tensor(s_tmp[:, 1:2], s_tmp[:, 0:1], i_sb[:, 0:1], ALU.add)
                ve.drain()
                ve.tensor_scalar(s_nxt[:, 0, b:b + 1], s_tmp[:, 1:2], 2.0, None, ALU.mult)
                ve.tensor_scalar(s_nxt[:, 1, b:b + 1], s_tmp[:, 1:2], 2.0, 1.0, ALU.mult, ALU.add).then_inc(idx_ok, 1)

            def x_lo(b, ix):
                for half in range(2):
                    ve.wait_ge(x_h, ix * 2 + (half + 1))
                    ve.tensor_tensor(xT_lo[b][:, 4 * half:4 * half + 4, :], bank(6 + half).rearrange("p (k n) -> p k n", n=P),
                                     xT_hi[b][:, 4 * half:4 * half + 4, :].bitcast(F32), ALU.subtract).then_inc(x_l, 1)

            passes = ve.value_load(tab[0:1, 4 * TABW:4 * TABW + 1], min_val=1, max_val=TABW - 2)
            n0 = ve.value_load(tab[0:1, TABW + 1:TABW + 2], min_val=1, max_val=MAXB)
            e0 = ve.value_load(tab[0:1, 1:2], min_val=0, max_val=E - 1)
            slots_of(e0, pbase[:, 1:2])
            ve.tensor_copy(s_nxt[:].rearrange("p h b -> p (h b)"), ones[:, 0:2 * MAXB])
            ve.tensor_copy(gt_nxt[:], ones[:, 0:MAXB])
            ve.drain()
            mark(0, 0, True)
            write_lo(ve, X_CH % 2, X_CH % 2, X_CH + 1, slice(0, V_KT), s_lo)
            indices(0, 0)
            for b in range(1, MAXB):
                with ve.If(n0 > b):
                    mark(b, b, True)
                    indices(b, b)
            x_lo(0, 0)
            for b in range(1, MAXB):
                with ve.If(n0 > b):
                    x_lo(b, b)

            with ve.Fori(0, passes) as p:
                n = ve.value_load(tab[0:1, bass.ds(p + (TABW + 1), 1)], min_val=1, max_val=MAXB)
                n2 = ve.value_load(tab[0:1, bass.ds(p + (TABW + 2), 1)], min_val=0, max_val=MAXB)
                B = ve.value_load(tab[0:1, bass.ds(p + (2 * TABW + 1), 1)], min_val=0, max_val=64)
                e2 = ve.value_load(tab[0:1, bass.ds(p + 2, 1)], min_val=0, max_val=E - 1)

                def add_bias(c_, b):
                    ve.drain()
                    if b == 0:
                        slot = (X_CH + c_) % 3
                        landed = p * (48, 64, 48)[slot] + {0: 32, 3: 64, 1: 32, 4: 48, 2: 32, 5: 48}[c_]
                        ve.wait_ge(s_bias[slot], landed)
                    ve.wait_ge(m_done, B * NPC + n * c_ + (b + 2))
                    src = bank(u_bank[b][c_ % 2])
                    ve.tensor_tensor(ut[:], src, bias[(X_CH + c_) % 3][:], ALU.add).then_inc(m_free, 1)
                    ve.drain()

                def act_lo(c_, b):
                    ve.wait_ge(aT_h, B * 4 + n * c_ + (b + 2))
                    ve.tensor_tensor(aT_lo[b][:, 2 * c_:2 * c_ + 2, :], bank(5)[:, 0:2 * P].rearrange("p (k n) -> p k n", n=P),
                                     aT_hi[b][:, 2 * c_:2 * c_ + 2, :].bitcast(F32), ALU.subtract).then_inc(aT_l, 1)

                def swiglu(c_, b):
                    add_bias(c_, b)
                    ve.tensor_scalar(ut[:, 0:SQ], ut[:, 0:SQ], LIMIT, None, ALU.min).then_inc(glu_ok, 1)
                    ve.tensor_scalar(ut[:, SQ:], ut[:, SQ:], LIMIT, -LIMIT, ALU.min, ALU.max)
                    ve.drain()
                    ve.scalar_tensor_tensor(ut[:, SQ:], ut[:, SQ:], 1.0, ut[:, 0:SQ], ALU.add, ALU.mult)
                    if c_:
                        act_lo(c_ - 1, b)
                    ve.drain()
                    ve.wait_ge(sig_ok, B * 4 + n * c_ + (b + 1))
                    ve.tensor_tensor(act_r[b][:], ut[:, SQ:], sg[:], ALU.mult).then_inc(act_ok, 1)

                def scale_out(c_, b):
                    add_bias(c_, b)
                    iy = B * 2 + n * (c_ - 4) + b
                    ve.wait_ge(y_out, iy * 16 + (16 if b == 0 else 0))
                    h = c_ - 4
                    ve.scalar_tensor_tensor(yst[(b + c_) % 2][:], ut[:], gt_cur[:, b:b + 1], g2_row[:, h * CW:(h + 1) * CW],
                                            ALU.mult, ALU.mult).then_inc(y_ok, 1)

                def block_step(c_, b):
                    if c_ == 4:
                        act_lo(3, b)
                    if c_ < 4:
                        swiglu(c_, b)
                    else:
                        scale_out(c_, b)

                def next_lo(c_):
                    ve.wait_ge(m_done, B * NPC + n * c_ + 1)
                    slot = (X_CH + c_ + 1) % 2
                    write_lo(ve, slot, slot, p * NPC + (X_CH + c_ + 2), slice(0, V_KT), s_lo)

                for c_ in range(NPC):
                    if 2 <= c_:
                        with ve.If(n2 > c_ - 2):
                            indices(c_ - 2, B + n + (c_ - 2))
                    if c_ < NPC - 1:
                        next_lo(c_)
                    else:
                        with ve.If(n2 > 0):
                            next_lo(c_)
                    for b in range(MAXB):
                        if c_ == NPC - 1:
                            with ve.If(n2 > b):
                                x_lo(b, B + n + b)
                        if b:
                            with ve.If(n > b):
                                block_step(c_, b)
                        else:
                            block_step(c_, b)
                    if c_ == 0:
                        ve.wait_ge(i_ps, B + n)
                        slots_of(e2, pbase[:, bass.ds(p + 2, 1)])
                        ve.drain()
                    if c_ < 4:
                        with ve.If(n2 > c_):
                            mark(c_, B + n + c_, False)
                    if c_ == 1:
                        ve.wait_ge(y_out, B * 32 + 16)
                        ve.tensor_copy(s_cur[:], s_nxt[:])
                        ve.tensor_copy(gt_cur[:], gt_nxt[:])
                        ve.drain()


_ARGS = ("x", "c", "ada_w", "ada_b", "norm1_g", "w_in", "conv_w", "conv_b", "conv_ln_g", "conv_ln_b", "q_norm_g",
         "k_norm_g", "rel_bias", "w_out", "norm2_g", "router_w", "router_b", "exp_w1", "exp_b1", "exp_w2", "exp_b2")


def kernel(**inputs):
    import numpy as np
    import concourse.bacc as _bacc
    from concourse.bass_utils import run_bass_kernel_spmd as _run

    nc = _bacc.Bacc("TRN2", target_bir_lowering=False, num_devices=1)
    arrays = {}
    for name in _ARGS:
        a = np.ascontiguousarray(inputs[name])
        arrays["in_" + name] = a if name == "c" else a[0]
    arrays["in_consts"] = make_consts()
    args = [nc.dram_tensor(name, a.shape, F32, kind="ExternalInput").ap() for name, a in arrays.items()]
    rel_ext = nc.dram_tensor("rel_ext", (NH, 384), F32, kind="Internal").ap()
    mod_dram = nc.dram_tensor("mod_dram", (4 * D,), F32, kind="Internal").ap()
    h2_dram = nc.dram_tensor("h2_dram", (T, D), F32, kind="Internal").ap()
    out = nc.dram_tensor("out", (T + P, D), F32, kind="ExternalOutput").ap()
    layer(nc, *args, rel_ext, mod_dram, h2_dram, out)
    r = _run(nc, [arrays], core_ids=[0])
    return np.asarray(r.results[0]["out"])[:T].reshape(1, T, D)
```

```python
from contextlib import ExitStack

import concourse.bass as bass
from concourse import mybir

F32 = mybir.dt.float32
F32R = mybir.dt.float32r
I32 = mybir.dt.int32
U32 = mybir.dt.uint32
ACT = mybir.ActivationFunctionType
ALU = mybir.AluOpType
AX_X = mybir.AxisListType.X

P = 128
T = 1024
D = 1024
TT = T // P
KT = D // P
CW = 512
CT = 512 // P
KC = 31
NH, HD = 8, 64
E = 32
TOPK = 4
MAXB = 4
SPLITS = T // (MAXB * P)
CAND = E * SPLITS
TABW = 44
EPS = 1e-6
NEG = -1e30
ALPHA, LIMIT = 1.702, 7.0
A_CH, GT_CH, K_CH, V_CH, Q_CH, O_CH, X_CH = 0, 1, 2, 3, 4, 5, 7
W_IN_COL = [0, 512, 1536, 2048, 1024]
NPC = 6
V_KT = (slice(0, 3), slice(4, 5))
P_KT = (slice(3, 4), slice(5, 8))
HK = KT // 2
SQ = 256

C_ID, C_ONE, C_COL, C_FAR, C_NEAR = 0, 128, 256, 272, 656
C_TRI, C_STRI, C_RM1, C_THR, C_VAL, C_IOTA = 912, 1040, 1104, 1148, 1152, 1154
C_SEL = C_IOTA + P
N_CONST = C_SEL + 512
V_C, V_G1, V_ADA, V_CB, V_LG, V_LB, N_VEC = 0, 8, 16, 32, 36, 40, 44


def make_consts():
    import numpy as np
    c = np.zeros((P, N_CONST), np.float32)
    p = np.arange(P)
    c[:, C_ID:C_ID + P] = np.eye(P)
    c[:, C_ONE:C_ONE + P] = 1
    c[:, C_COL:C_COL + 8] = p[:, None] + P * np.arange(8)
    c[:, C_COL + 8] = T + p
    c[:, C_COL + 9] = -(T + p)
    c[:, C_COL + 10] = EPS
    c[:, C_COL + 11] = HD * EPS
    c[64:, C_FAR:C_FAR + 64] = NEG
    c[:64, C_NEAR:C_NEAR + 64] = NEG
    c[:, C_TRI:C_TRI + P] = p[:, None] <= p[None, :]
    c[:64, C_STRI:C_STRI + 64] = p[:64, None] < p[None, :64]
    c[:, C_RM1:C_RM1 + TABW] = np.arange(TABW) - 1
    c[:, C_THR:C_THR + MAXB] = MAXB * P * (p % SPLITS)[:, None] + P * np.arange(MAXB)
    c[:, C_VAL] = p // SPLITS
    c[:, C_VAL + 1] = MAXB * P * (p % SPLITS)
    c[:, C_IOTA:C_SEL] = np.arange(P)
    c[:NH, C_SEL:] = np.arange(NH)[:, None] == np.arange(512) // HD
    return c


def layer(nc, x, c, ada_w, ada_b, norm1_g, w_in, conv_w, conv_b, ln_g, ln_b, q_g, k_g, rel_bias, w_out,
          norm2_g, router_w, router_b, w1, b1, w2, b2, consts, rel_ext, mod_dram, h2_dram, out):
    with ExitStack() as ctx:
        base = (nc.sbuf_base + 31) // 32 * 32
        KB = 1024

        def size(shape):
            n = 4
            for s in shape[1:]:
                n *= s
            return n

        def at(name, shape, off, dt=F32):
            assert off % 32 == 0 and base + off + size(shape) <= nc.sbuf_usable_end, (name, off + size(shape))
            return nc.alloc_sbuf_tensor_at(name, shape, dt, offset=base + off)

        def sem(name):
            return ctx.enter_context(nc.semaphore(name))

        def view(ap, dims, offset=0):
            return bass.AP(ap.tensor, ap.offset + offset, [list(ap.ap[0])] + dims)

        OPND, WORK = 96 * KB, 160 * KB
        TAB = WORK + 37376
        SMALL = TAB + 8 * KB
        stage = [at("stage0", [P, KT, CW], 0), at("stage1", [P, KT, CW], 16 * KB)]
        w_hi = [at("w_hi0", [P, KT, CW], 32 * KB, F32R), at("w_hi1", [P, KT, CW], 64 * KB, F32R)]
        w_lo = [at("w_lo0", [P, KT, CW], 48 * KB, F32R), at("w_lo1", [P, KT, CW], 80 * KB, F32R)]
        cst = at("cst", [P, C_FAR], SMALL)
        ident, ones = cst[:, C_ID:C_ID + P], cst[:, C_ONE:C_ONE + P]
        tok_id = cst[:, C_COL:C_COL + 8]
        pad_id, neg_pad = cst[:, C_COL + 8:C_COL + 9], cst[:, C_COL + 9:C_COL + 10]
        eps_col, eps64_col = cst[:, C_COL + 10:C_COL + 11], cst[:, C_COL + 11:C_COL + 12]
        spot = [SMALL + 4 * C_FAR]

        def tiny(name, shape, dt=F32):
            t = at(name, shape, spot[0], dt)
            spot[0] += (size(shape) + 31) // 32 * 32
            return t

        x_rows = at("x_rows", [P, TT, D], 64 * KB)
        ada_t = [at("ada0", [P, 2048], 16 * KB), at("ada1", [P, 2048], 24 * KB)]
        ada_first = at("ada_first", [P, KT, 2048], OPND)
        ada_acc = at("ada_acc", [P, 2048], WORK + 16896)
        mod_row = at("mod_row", [1, 2048], WORK + 16896 + 8 * KB)
        h_full = [at("h_full0", [P, T], WORK), at("h_full1", [P, T], WORK + 4 * KB)]
        op_hi = at("op_hi", [P, KT, T], OPND, F32R)
        op_lo = at("op_lo", [P, KT, T], OPND + 32 * KB, F32R)
        uT = at("uT", [P, CT, KC - 1 + T], WORK)
        kT = at("kT", [P, 4, T], WORK + 16896)
        acc = at("acc", [P, T], WORK + 33280)
        sig_t = [at("sig_t0", [P, CW], WORK + 33280), at("sig_t1", [P, CW], WORK + 35328)]
        v_rows = at("v_rows", [P, TT, 512], 16 * KB)
        k_sq = at("k_sq", [P, 512], 16 * KB)
        k_row = at("k_row", [P, 512], 18 * KB)
        qT = at("qT", [P, KT, T], OPND)
        q_tmp = at("q_tmp", [P, KT, T], OPND + 32 * KB)
        rel_rows = at("rel_rows", [NH, 384], TAB)
        vec_rows = at("vec_rows", [N_VEC, P], TAB + 2 * KB)
        tap_rows = at("tap_rows", [KC, 512], TAB + 4 * KB)
        near_bias = at("near_bias", [P, NH, 256], TAB)
        s_sb = [at(f"s_sb{i}", [P, 640], (OPND + 32 * KB, OPND + 32 * KB + 2560, 32 * KB)[i]) for i in range(3)]
        p_T = [at(f"p_T{i}", [P, 640], OPND + 37 * KB + 2560 * i) for i in range(2)]
        y_sb = at("y_sb", [P, 512], OPND + 42 * KB)
        head_of = at("head_of", [NH, 512], 35 * KB)
        r_T = at("r_T", [NH, P], 37 * KB)
        masks = at("masks", [P, 640], OPND + 44 * KB)
        taps = tiny("taps", [P, CT, KC])
        gains = tiny("gains", [P, 2, HD])
        stat = tiny("stat", [P, 16])
        sq_sum = tiny("sq_sum", [P, 8])
        sq_root = tiny("sq_root", [P, 8])
        sq_inv = tiny("sq_inv", [P, 8])
        mx = tiny("mx", [P, 12])
        rsum = tiny("rsum", [P, 16])
        r_inv = tiny("r_inv", [P, 8])
        cols = tiny("cols", [P, N_VEC])
        c_act = tiny("c_act", [P, 16])
        mod_col = tiny("mod_col", [P, 16])
        ln_a = at("ln_a", [P, T], 16 * KB)
        ln_t = at("ln_t", [P, T], 20 * KB)
        ln_r = at("ln_r", [P, T], 24 * KB)
        ln_z = at("ln_z", [P, T], 28 * KB)
        ln_sq = lambda t: (ln_a, ln_t)[t % 2]
        ln_sig = lambda t: (ln_z, ln_a)[t % 2]
        x2 = at("x2", [P, TT, D], WORK)
        g1_row = at("g1_row", [P, D], 16 * KB)
        a2_row = at("a2_row", [P, D], 20 * KB)
        sh2_row = at("sh2_row", [P, D], 24 * KB)
        t_row = [at("t_row0", [P, CW], 28 * KB), at("t_row1", [P, CW], 30 * KB)]
        h2r = at("h2r", [P, KT, T], OPND)
        h2T = at("h2T", [P, KT, T], OPND + 32 * KB)
        rw = at("rw", [P, KT, E], WORK + 32 * KB)
        rb_row = at("rb_row", [P, E], WORK + 33 * KB)
        n2_row = at("n2_row", [P, D], TAB + 4 * KB)
        R = OPND
        lgt = at("lgt", [P, TT, E], WORK + 33 * KB + 128)
        top = at("top", [P, TT, 8], WORK + 34 * KB + 128)
        top_i = at("top_i", [P, TT, 8], WORK + 34 * KB + 384, U32)
        top_f = at("top_f", [P, TT, 8], WORK + 34 * KB + 640)
        consts2 = at("consts2", [P, C_IOTA - C_TRI], R)
        tri = consts2[:, 0:P]
        stri = consts2[0:CAND, C_STRI - C_TRI:C_STRI - C_TRI + CAND]
        row_m1 = consts2[0:CAND, C_RM1 - C_TRI:C_RM1 - C_TRI + TABW]
        thr = consts2[0:CAND, C_THR - C_TRI:C_THR - C_TRI + MAXB]
        cand_val = consts2[0:CAND, C_VAL - C_TRI:C_VAL - C_TRI + 2]
        gex = at("gex", [P, TT, TOPK], R + 2 * KB)
        gsum = at("gsum", [P, TT], R + 2 * KB + 128)
        ginv = at("ginv", [P, TT], R + 2 * KB + 192)
        hot = at("hot", [P, TOPK, TT, E], R + 16 * KB)
        hotg = at("hotg", [P, TT, E], R + 4 * KB)
        mask = at("mask", [P, TT, E], R + 5 * KB)
        gate_te = at("gate_te", [P, TT, E], R + 6 * KB)
        rank = at("rank", [P, TT, E], R + 7 * KB)
        pre = at("pre", [P, TT, E], R + 8 * KB)
        mask2 = at("mask2", [P, TT, CAND], R + 14 * KB)
        cmp = at("cmp", [CAND, MAXB], R + 9 * KB)
        cand = at("cand", [CAND, 8], R + 9 * KB + 32)
        sel = at("sel", [CAND, TABW], R + 10 * KB)
        base_rep = at("base_rep", [CAND, P], R + 11 * KB)
        xT_hi = [at(f"xT_hi{b}", [P, KT, P], OPND + 4 * KB * b, F32R) for b in range(MAXB)]
        xT_lo = [at(f"xT_lo{b}", [P, KT, P], OPND + 16 * KB + 4 * KB * b, F32R) for b in range(MAXB)]
        aT_hi = [at(f"aT_hi{b}", [P, KT, P], OPND + 32 * KB + 4 * KB * b, F32R) for b in range(MAXB)]
        aT_lo = [at(f"aT_lo{b}", [P, KT, P], OPND + 48 * KB + 4 * KB * b, F32R) for b in range(MAXB)]
        xg = [at(f"xg{b}", [P, D], WORK + 4 * KB * b) for b in range(MAXB)]
        yst = [at(f"yst{b}", [P, CW], WORK + 16 * KB + 2 * KB * b) for b in range(2)]
        bias = [at(f"bias{b}", [P, CW], WORK + 20 * KB + 2 * KB * b) for b in range(3)]
        onehot = at("onehot", [P, TT, P], WORK + 26 * KB, F32R)
        ut = at("ut", [P, CW], WORK + 30 * KB)
        sg = at("sg", [P, SQ], WORK + 32 * KB)
        act_r = [at(f"act_r{b}", [P, SQ], WORK + 33 * KB + KB * b) for b in range(3)]
        g2_row = at("g2_row", [P, D], TAB)
        pos_et = at("pos_et", [P, E, TT], TAB + 4 * KB)
        gate_et = at("gate_et", [P, E, TT], TAB + 5 * KB)
        iota = at("iota", [P, P], TAB + 6 * KB)
        act_r.append(at("act_r3", [P, SQ], TAB + 6 * KB + 512))
        spot[0] = SMALL + 4 * C_FAR
        tab = tiny("tab", [1, 5 * TABW], I32)
        pbase = tiny("pbase", [P, TABW])
        posr = tiny("posr", [P, TT])
        posb = tiny("posb", [P, TT])
        rhs = tiny("rhs", [P, TT, 4], F32R)
        g_idx = tiny("g_idx", [P, MAXB], U32)
        s_nxt = tiny("s_nxt", [P, 2, MAXB], U32)
        s_cur = tiny("s_cur", [P, 2, MAXB], U32)
        gt_nxt = tiny("gt_nxt", [P, MAXB])
        gt_cur = tiny("gt_cur", [P, MAXB])
        s_tmp = tiny("s_tmp", [P, MAXB])
        i_sb = tiny("i_sb", [P, 4])
        keep = tiny("keep", [P, 1])

        pair = [ctx.enter_context(nc.psum_tensor(f"pair{i}", [P, 2 * CW], F32)) for i in range(4)]

        def bank(i):
            return pair[i // 2][:, i % 2 * CW:(i % 2 + 1) * CW]

        s_cst, s_vec, s_tap, s_relrow, s_gain = (sem(n) for n in ("s_cst", "s_vec", "s_tap", "s_relrow", "s_gain"))
        s_x = [sem("s_x0"), sem("s_x1")]
        s_ada_first = [sem(f"s_ada_first{i}") for i in range(KT // 2)]
        s_ada = [sem("s_ada0"), sem("s_ada1")]
        s_adab = sem("s_adab")
        s_stage = [[sem(f"s_stage{i}{h}") for h in range(2)] for i in range(2)]
        s_hi, s_lo, s_plo = sem("s_hi"), sem("s_lo"), sem("s_plo")
        s_vecT, s_cols, s_csig = sem("s_vecT"), sem("s_cols"), sem("s_csig")
        s_tapT, s_taps = sem("s_tapT"), sem("s_taps")
        s_xroot, s_xn = sem("s_xroot"), sem("s_xn")
        s_adastep, s_modp, s_modc, s_modr, s_modst = (sem(n) for n in ("s_adastep", "s_modp", "s_modc", "s_modr", "s_modst"))
        s_modfree = sem("s_modfree")
        s_xT, s_hfull, s_hhi, s_hlo = sem("s_xT"), sem("s_hfull"), sem("s_hhi"), sem("s_hlo")
        s_tile, s_tfree = sem("s_tile"), sem("s_tfree")
        s_gsig, s_uz = sem("s_gsig"), sem("s_uz")
        s_qsq, s_qss, s_qroot, s_qn, s_qkT, s_qkev = (sem(n) for n in ("s_qsq", "s_qss", "s_qroot", "s_qn", "s_qkT", "s_qkev"))
        s_dve = sem("s_dve")
        s_relst, s_relld, s_mask = sem("s_relst"), sem("s_relld"), sem("s_mask")
        s_rel, s_head = sem("s_rel"), sem("s_head")
        s_S, s_Sfree, s_nmx, s_exp, s_PT, s_pTc, s_PV, s_y, s_yhi, s_ylo = (
            sem(n) for n in ("s_S", "s_Sfree", "s_nmx", "s_exp", "s_PT", "s_pTc", "s_PV", "s_y", "s_yhi", "s_ylo"))
        s_rinv, s_rT, s_rTc, s_rep = (sem(n) for n in ("s_rinv", "s_rT", "s_rTc", "s_rep"))
        s_lnsum, s_lnc, s_lnsq, s_lnvar, s_lnroot, s_lnz, s_lnsig, s_lny, s_lnhi, s_lnlo = (
            sem(n) for n in ("s_lnsum", "s_lnc", "s_lnsq", "s_lnvar", "s_lnroot", "s_lnz", "s_lnsig", "s_lny", "s_lnhi", "s_lnlo"))
        s_x2ld, s_rows = [sem(f"s_x2ld{i}") for i in range(TT)], sem("s_rows")
        s_x2, s_x2root, s_h2, s_h2T, s_h2Tc, s_lg = (
            sem(n) for n in ("s_x2", "s_x2root", "s_h2", "s_h2T", "s_h2Tc", "s_lg"))
        s_h2st, s_outst, s_c2 = sem("s_h2st"), sem("s_outst"), sem("s_c2")
        s_nm, s_gex, s_mk, s_rk, s_cn, s_cv, s_pf, s_sl, s_tb, s_tab, s_iota = (
            sem(n) for n in ("s_nm", "s_gex", "s_mk", "s_rk", "s_cn", "s_cv", "s_pf", "s_sl", "s_tb", "s_tab", "s_iota"))
        m_done = sem("m_done")
        m_free = sem("m_free")
        glu_ok, sig_ok, act_ok = sem("glu_ok"), sem("sig_ok"), sem("act_ok")
        aT_ps, aT_h, aT_l = sem("aT_ps"), sem("aT_h"), sem("aT_l")
        oh_ok, i_ps, idx_ok = sem("oh_ok"), sem("i_ps"), sem("idx_ok")
        g_in, x_ps, x_h, x_l = sem("g_in"), sem("x_ps"), sem("x_h"), sem("x_l")
        g_go, y_go = sem("g_go"), sem("y_go")
        y_ok, y_out = sem("y_ok"), sem("y_out")
        s_bias = [sem(f"s_bias{i}") for i in range(3)]

        w_in_v = w_in.rearrange("(k p) n -> p k n", p=P)
        w_out_v = w_out.rearrange("(k p) n -> p k n", p=P)
        w1_v = w1.rearrange("e (k p) (s n) -> e p k s n", p=P, s=2)
        w2_v = w2.rearrange("e (k p) n -> e p k n", p=P)
        out_half = out.rearrange("t (h n) -> (t h) n", h=2)
        u_bank = [(0, 1), (2, 2), (3, 3), (4, 4)]
        N_QK = 2 * TT

        def halves(N, h, p=None):
            return 2 * N + h + 1 if p is None else p * (2 * NPC) + (2 * N + h + 1)

        def write_hi(act, par, slot, seen, which=(0, 1)):
            for h in which:
                tiles = slice(HK * h, HK * h + HK)
                act.wait_ge(s_stage[slot][h], seen)
                act.activation(w_hi[par][:, tiles, :], stage[slot][:, tiles, :], ACT.Copy).then_inc(s_hi, 1)

        def write_lo(eng, par, slot, N, p, tiles, done, which=(0, 1)):
            for h in which:
                eng.wait_ge(s_hi, halves(N, h, p))
                eng.tensor_tensor(w_lo[par][:, tiles[h], :], stage[slot][:, tiles[h], :], w_hi[par][:, tiles[h], :].bitcast(F32),
                                  ALU.subtract).then_inc(done, 1)

        def before_trunk_split(eng, C):
            if C == 1:
                eng.wait_ge(s_xT, KT)
            elif C >= 2:
                eng.wait_ge(s_tile, 8 * (C - 1))

        class Passes:
            def __init__(self, eng):
                self.eng = eng
                self.count = eng.value_load(tab[0:1, 4 * TABW:4 * TABW + 1], min_val=1, max_val=TABW - 2)
                self.n0 = eng.value_load(tab[0:1, TABW + 1:TABW + 2], min_val=1, max_val=MAXB)
                self.regs = [eng.alloc_register(f"{r}_{eng.engine.name}") for r in ("last", "now", "before", "used")]
                for reg, v in zip(self.regs, (0, self.n0, 0, 0)):
                    eng.reg_mov(reg, v)

            def begin(self, p):
                last, now, before, used = self.regs
                snap = self.eng.snap
                self.n_p, self.n = snap(last, min_val=0, max_val=MAXB), snap(now, min_val=1, max_val=MAXB)
                self.B, self.w0 = snap(before, min_val=0, max_val=64), snap(used, min_val=0, max_val=512)
                self.n2 = self.eng.value_load(tab[0:1, bass.ds(p + (TABW + 2), 1)], min_val=0, max_val=MAXB)
                return self.n, self.n2, self.B

            def end(self):
                last, now, before, used = self.regs
                self.eng.reg_mov(last, self.n)
                self.eng.reg_mov(now, self.n2)
                self.eng.reg_mov(used, self.B * NPC + self.n * 4 + 1)
                self.eng.reg_mov(before, self.B + self.n)

        block = ctx.enter_context(nc.Block())

        @block.sync
        def _(sp):
            sp.dma_start(cst[:], consts[:, 0:C_FAR]).then_inc(s_cst, 16)
            sp.dma_start(vec_rows[V_C:V_C + 8, :], c.rearrange("a (k p) -> (a k) p", p=P)).then_inc(s_vec, 16)
            sp.dma_start(vec_rows[V_G1:V_G1 + 8, :], norm1_g.rearrange("(k p) -> k p", p=P)).then_inc(s_vec, 16)
            sp.dma_start(vec_rows[V_ADA:V_ADA + 16, :], ada_b[0:2048].rearrange("(k p) -> k p", p=P)).then_inc(s_vec, 16)
            for v, n in ((conv_b, V_CB), (ln_g, V_LG), (ln_b, V_LB)):
                sp.dma_start(vec_rows[n:n + 4, :], v.rearrange("(k p) -> k p", p=P)).then_inc(s_vec, 16)
            sp.dma_start(tap_rows[:], conv_w).then_inc(s_tap, 16)
            xv = x.rearrange("(i p) d -> p i d", p=P)
            for h in range(2):
                sp.dma_start(x_rows[:, 4 * h:4 * h + 4, :], xv[:, 4 * h:4 * h + 4, :]).then_inc(s_x[h], 16)
            sp.dma_start(rel_rows[:, 0:257], rel_bias).then_inc(s_relrow, 16)
            for i in range(KT // 2):
                sp.dma_start(ada_first[:, 2 * i:2 * i + 2, :], ada_w[2 * i * P:(2 * i + 2) * P, 0:2048].rearrange("(k p) n -> p k n", p=P)
                             ).then_inc(s_ada_first[i], 16)
            for h in range(2):
                sp.dma_start(stage[0][:, HK * h:HK * h + HK, :], w_in_v[:, HK * h:HK * h + HK, 0:CW]).then_inc(s_stage[0][h], 16)
            sp.dma_start(gains[:, 0, :], q_g.partition_broadcast(P)).then_inc(s_gain, 16)
            sp.dma_start(gains[:, 1, :], k_g.partition_broadcast(P)).then_inc(s_gain, 16)
            sp.wait_ge(s_rel, 1)
            sp.dma_start(rel_ext, rel_rows[:]).then_inc(s_relst, 16)

            def load_chunk(C):
                src = w_in_v[:, :, W_IN_COL[C]:W_IN_COL[C] + CW] if C < O_CH else w_out_v[:, :, (C - O_CH) * CW:(C - O_CH + 1) * CW]
                for h in range(2):
                    sp.wait_ge(s_lo, halves(C - 1, h))
                    sp.wait_ge(s_plo, halves(C - 1, h))
                    sp.dma_start(stage[0][:, HK * h:HK * h + HK, :], src[:, HK * h:HK * h + HK, :]).then_inc(s_stage[0][h], 16)

            load_chunk(1)
            sp.wait_ge(s_relst, 16)
            sp.wait_ge(s_cols, 1)
            sp.wait_ge(s_taps, 1)
            for h in range(NH):
                sp.dma_start(near_bias[:, h, :], bass.AP(rel_ext.tensor, rel_ext.offset + 384 * h + 1, [[1, P], [1, 256]])).then_inc(s_relld, 16)
            load_chunk(2)
            for half in range(2):
                sp.wait_ge(s_modr, half + 1)
                sp.dma_start(mod_dram[2048 * half:2048 * half + 2048].rearrange("(a n) -> a n", a=1), mod_row[:]).then_inc(s_modst, 16)
            load_chunk(3)
            load_chunk(4)
            load_chunk(5)
            sp.wait_ge(s_tile, 8 * 5)
            sp.wait_ge(s_qkT, N_QK)
            sp.dma_start(masks[:], consts[:, C_FAR:C_FAR + 640]).then_inc(s_mask, 16)
            sp.dma_start(head_of[:], consts[0:NH, C_SEL:C_SEL + 512]).then_inc(s_head, 16)
            load_chunk(6)
            sp.wait_ge(s_modst, 32)
            sp.wait_ge(s_S, NH * TT)
            sp.wait_ge(s_dve, CT * KC)
            for i in range(TT // 2 + 1, TT):
                sp.dma_start(x2[:, i, :], x[i * P:(i + 1) * P, :]).then_inc(s_x2ld[i], 16)
            sp.wait_ge(s_lnhi, CT)
            sp.wait_ge(s_lnlo, CT)
            sp.wait_ge(s_ylo, TT)
            for i in range(TT // 2 + 1):
                sp.dma_start(x2[:, i, :], x[i * P:(i + 1) * P, :]).then_inc(s_x2ld[i], 16)
            for rows, src in ((g1_row, mod_dram[0:1024]), (a2_row, mod_dram[2048:3072]), (n2_row, norm2_g), (sh2_row, mod_dram[1024:2048]),
                              (rb_row, router_b), (g2_row, mod_dram[3072:4096])):
                sp.dma_start(rows[:], src.partition_broadcast(P)).then_inc(s_rows, 16)
            sp.dma_start(rw[:], router_w.rearrange("(k p) e -> p k e", p=P)).then_inc(s_rows, 16)
            for i in range(TT):
                sp.wait_ge(s_h2, i + 1)
                sp.dma_start(out[i * P:(i + 1) * P, :], x2[:, i, :]).then_inc(s_outst, 16)
                sp.dma_start(h2_dram[i * P:(i + 1) * P, :].rearrange("p (k f) -> p k f", f=P),
                             h2r[:, :, i * P:(i + 1) * P]).then_inc(s_h2st, 16)
            sp.wait_ge(s_lg, TT)
            sp.wait_ge(s_h2st, 16 * TT)
            sp.wait_ge(s_tile, 8 * X_CH)
            sp.dma_start(consts2[:], consts[:, C_TRI:C_IOTA]).then_inc(s_c2, 16)
            sp.dma_start(iota[:], consts[:, C_IOTA:C_IOTA + P]).then_inc(s_iota, 16)

            sp.wait_ge(s_tab, 1)
            ps = Passes(sp)
            with sp.Fori(0, ps.count) as p:
                ex = sp.value_load(tab[0:1, bass.ds(p + 1, 1)], min_val=0, max_val=E - 1)
                n, n2, B = ps.begin(p)
                n_p, w0 = ps.n_p, ps.w0

                def weights(c):
                    slot = (X_CH + c) % 2
                    for h in range(2):
                        sp.wait_ge(s_lo, halves(X_CH + c - 2, h, p))
                        sp.wait_ge(s_plo, halves(X_CH + c - 2, h, p))
                        kt = slice(HK * h, HK * h + HK)
                        if c < 4:
                            for s in range(2):
                                sp.dma_start(stage[slot][:, kt, s * SQ:(s + 1) * SQ],
                                             w1_v[bass.ds(ex, 1), :, kt, s, c * SQ:(c + 1) * SQ].rearrange("e p k n -> (e p) k n")
                                             ).then_inc(s_stage[slot][h], 16)
                        else:
                            sp.dma_start(stage[slot][:, kt, :],
                                         w2_v[bass.ds(ex, 1), :, kt, (c - 4) * CW:(c - 3) * CW].rearrange("e p k n -> (e p) k n")
                                         ).then_inc(s_stage[slot][h], 16)

                def biases(c):
                    if c >= 3:
                        sp.wait_ge(m_free, B * NPC + n * (c - 2) + 2)
                    else:
                        sp.wait_ge(m_free, w0 + n_p * c + 1)
                    if c < 4:
                        for s in range(2):
                            sp.dma_start(bias[(X_CH + c) % 3][:, s * SQ:(s + 1) * SQ],
                                         b1[bass.ds(ex, 1), s * D + c * SQ:s * D + (c + 1) * SQ].to_broadcast([P, SQ])
                                         ).then_inc(s_bias[(X_CH + c) % 3], 16)
                    else:
                        sp.dma_start(bias[(X_CH + c) % 3][:], b2[bass.ds(ex, 1), (c - 4) * CW:(c - 3) * CW].to_broadcast([P, CW])
                                     ).then_inc(s_bias[(X_CH + c) % 3], 16)

                weights(0)
                for c_ in range(1, NPC):
                    weights(c_)
                    biases(c_ - 1)
                biases(NPC - 1)
                ps.end()
            sp.wait_ge(s_outst, 16 * TT)

        @block.gpsimd
        def _(pool):
            def ada_loads(part):
                for k in range(KT):
                    n = part * KT + k
                    if n >= KT + 2:
                        pool.wait_ge(s_adastep, n - 1)
                    elif n == KT:
                        pool.wait_ge(s_adastep, 2)
                    pool.dma_start(ada_t[n % 2][:], ada_w[k * P:(k + 1) * P, part * 2048:(part + 1) * 2048]
                                   ).then_inc(s_ada[n % 2], 16)

            def lo_part(C):
                before_trunk_split(pool, C)
                write_lo(pool, C % 2, 0, C, None, P_KT, s_plo)

            lo_part(0)
            lo_part(1)
            pool.dma_start(mod_row[:], ada_b[2048:4096].rearrange("(a n) -> a n", a=1)).then_inc(s_adab, 16)
            ada_loads(1)
            lo_part(2)
            pool.wait_ge(s_modst, 16)
            pool.dma_start(mod_row[:], ada_b[4096:6144].rearrange("(a n) -> a n", a=1)).then_inc(s_adab, 16)
            ada_loads(2)
            lo_part(3)
            lo_part(4)
            lo_part(5)
            lo_part(6)
            pool.wait_ge(s_h2, 1)
            pool.dma_start(out[T:T + P, :], x2[:, 0, :]).then_inc(y_out, 16)
            pool.wait_ge(s_tab, 1)
            pool.wait_ge(s_h2st, 16 * TT)
            pool.wait_ge(s_outst, 16 * TT)

            def gather(b, ix, first, B=None, n=None):
                pool.wait_ge(idx_ok, ix + 1)
                if not first or b:
                    pool.wait_ge(g_in, 16 * ix if first else ix * 16)
                if not first:
                    pool.wait_ge(x_ps, B * 2 + n * 2)
                pool.sem_inc(g_go, 1)
                pool.indirect_dma_start(xg[b][:], None, h2_dram, bass.IndirectOffsetOnAxis(ap=g_idx[:, b:b + 1], axis=0)
                                        ).then_inc(g_in, 16)

            ps = Passes(pool)
            n0 = ps.n0
            gather(0, 0, True)
            write_lo(pool, X_CH % 2, X_CH % 2, X_CH, None, P_KT, s_plo)
            for b in range(1, MAXB):
                with pool.If(n0 > b):
                    gather(b, b, True)
            with pool.Fori(0, ps.count) as p:
                n, n2, B = ps.begin(p)
                for c_ in range(NPC):
                    def next_lo():
                        slot = (X_CH + c_ + 1) % 2
                        write_lo(pool, slot, slot, X_CH + c_ + 1, p, P_KT, s_plo)
                    if c_ < NPC - 1:
                        next_lo()
                    else:
                        with pool.If(n2 > 0):
                            next_lo()
                    if c_ >= 2:
                        with pool.If(n2 > c_ - 2):
                            gather(c_ - 2, B + n + (c_ - 2), False, B, n)
                    if c_ >= 4:
                        for b in range(MAXB):
                            def scatter():
                                iy = B * 2 + n * (c_ - 4) + b
                                pool.wait_ge(y_ok, iy + 1)
                                pool.wait_ge(y_out, iy * 16 + 16)
                                pool.sem_inc(y_go, 1)
                                pool.indirect_dma_start(
                                    out_half, bass.IndirectOffsetOnAxis(ap=s_cur[:, c_ - 4, b:b + 1], axis=0),
                                    yst[(b + c_) % 2][:], None, compute_op=ALU.add).then_inc(y_out, 16)
                            if b:
                                with pool.If(n > b):
                                    scatter()
                            else:
                                scatter()
                ps.end()
            end = pool.value_load(tab[0:1, 4 * TABW + 1:4 * TABW + 2], min_val=1, max_val=256)
            pool.wait_ge(y_out, end * 32 + 16)

        @block.tensor
        def _(pe):
            def half_ready(N, h, p=None):
                pe.wait_ge(s_hi, halves(N, h, p))
                pe.wait_ge(s_lo, halves(N, h, p))
                pe.wait_ge(s_plo, halves(N, h, p))

            def product(dst, a_hi, a_lo, b_hi, b_lo, kts, start, stop, new=None):
                for k in kts:
                    if new and k % HK == 0:
                        half_ready(new[0], k // HK, new[1])
                    for i, (u, v) in enumerate(((a_hi, b_hi), (a_hi, b_lo), (a_lo, b_hi))):
                        last = pe.matmul(dst, u(k), v(k), start=start and k == kts[0] and i == 0,
                                         stop=stop and k == kts[-1] and i == 2)
                return last

            pe.wait_ge(s_cst, 16)
            pe.wait_ge(s_vec, 16 * 6)
            pe.transpose(bank(6)[:, 0:N_VEC], vec_rows[:], ident[0:N_VEC, 0:N_VEC]).then_inc(s_vecT, 1)
            pe.wait_ge(s_tap, 16)
            for t in range(CT):
                last = pe.transpose(bank(7)[:, t * KC:(t + 1) * KC], tap_rows[:, t * P:(t + 1) * P], ident[0:KC, 0:KC])
            last.then_inc(s_tapT, 1)

            for k in range(KT):
                if k == 0:
                    pe.wait_ge(s_xn, TT)
                if k >= 2:
                    pe.wait_ge(s_hfull, k - 1)
                for i in range(TT):
                    last = pe.transpose(pair[k % 2][:, i * P:(i + 1) * P], x_rows[:, i, k * P:(k + 1) * P], ident)
                last.then_inc(s_xT, 1)
                if k == 1:
                    pe.wait_ge(s_adastep, KT)
                    pe.wait_ge(s_cols, 1)
                    for j in range(16):
                        last = pe.matmul(bank(6)[:, j:j + 1], ada_acc[:, j * P:(j + 1) * P], ones[:, 0:1], start=True, stop=True)
                    last.then_inc(s_modp, 1)

            def mod_rows(half):
                pe.wait_ge(s_adastep, KT * (half + 2))
                for j in range(4):
                    m = 4 * half + j
                    if m >= 2:
                        pe.wait_ge(s_modfree, m - 1)
                    else:
                        pe.wait_ge(s_modc, 1)
                        pe.wait_ge(s_taps, 1)
                    pe.matmul(bank(6 + m % 2)[0:1, :], ones[:, 0:1], ada_acc[:, j * CW:(j + 1) * CW],
                              start=True, stop=True).then_inc(s_modp, 1)

            def tile_begin(m):
                if m >= 4:
                    pe.wait_ge(s_tfree, m - 3)
                return bank(m % 4)

            def w(parts, C, n0=0, n1=CW):
                return lambda k: parts[C % 2][:, k, n0:n1]

            def rows_of(parts, i):
                return lambda k: parts[:, k, i * P:(i + 1) * P]

            pe.wait_ge(s_hlo, KT)
            pe.wait_ge(s_hhi, KT)
            for C in (A_CH, GT_CH):
                for t in range(CT):
                    for half in range(2):
                        m = C * 8 + t * 2 + half
                        dst = tile_begin(m)
                        tok = lambda parts: (lambda k: parts[:, k, half * CW:(half + 1) * CW])
                        product(dst, w(w_hi, C, t * P, t * P + P), w(w_lo, C, t * P, t * P + P), tok(op_hi), tok(op_lo),
                                range(KT), True, True, (C, None) if m % 8 == 0 else None).then_inc(s_tile, 1)
                mod_rows(C)

            def qk_transposes(j):
                pe.wait_ge(s_qn, j + 1)
                if j >= 2:
                    pe.wait_ge(s_qkev, j - 1)
                for g in range(4):
                    src = k_row[:, g * P:(g + 1) * P] if j < TT else q_tmp[:, g, (j - TT) * P:(j - TT + 1) * P]
                    last = pe.transpose(bank(4 + j % 2)[:, g * P:(g + 1) * P], src, ident)
                last.then_inc(s_qkT, 1)

            for C in (K_CH, V_CH, Q_CH):
                for i in range(TT):
                    m = C * 8 + i
                    dst = tile_begin(m)
                    product(dst, rows_of(op_hi, i), rows_of(op_lo, i), w(w_hi, C), w(w_lo, C), range(KT), True, True,
                            (C, None) if i == 0 else None).then_inc(s_tile, 1)
                    if C == K_CH and i:
                        qk_transposes(i - 1)
                    if C == V_CH and i == 0:
                        qk_transposes(TT - 1)
                    if C == Q_CH and i:
                        qk_transposes(TT + i - 1)
            qk_transposes(2 * TT - 1)
            pe.wait_ge(s_qkev, 2 * TT)

            units = [(j, h) for j in range(TT) for h in range(NH)]

            def scores(u):
                j, h = units[u]
                nk = min(j, 4) + 1
                if u >= 2:
                    pe.wait_ge(s_Sfree, u - 1)
                else:
                    pe.wait_ge(s_tfree, 8 * 5)
                lo, g = h % 2 * HD, h // 2
                for n0 in range(0, nk * P, CW):
                    n1 = min(n0 + CW, nk * P)
                    last = pe.matmul(pair[u % 2][:, n0:n1], qT[lo:lo + HD, g, j * P:(j + 1) * P],
                                     kT[lo:lo + HD, g, (j + 1 - nk) * P + n0:(j + 1 - nk) * P + n1], start=True, stop=True)
                last.then_inc(s_S, 1)

            def turn_probs(u):
                nk = min(units[u][0], 4) + 1
                pe.wait_ge(s_exp, u + 1)
                if u >= 1:
                    pe.wait_ge(s_pTc, u)
                if units[u][1] == 3 and units[u][0]:
                    pe.wait_ge(s_rTc, units[u][0])
                if units[u][1] == 4 and units[u][0]:
                    pe.wait_ge(s_y, units[u][0])
                for k in range(nk):
                    last = pe.transpose(pair[2][:, k * P:(k + 1) * P], s_sb[u % 3][:, k * P:(k + 1) * P], ident)
                last.then_inc(s_PT, 1)

            def weigh_values(u):
                j, h = units[u]
                nk = min(j, 4) + 1
                pe.wait_ge(s_pTc, u + 1)
                if h == 0 and j >= 2:
                    pe.wait_ge(s_y, j - 1)
                part, g = h % 2 * HD, h // 2
                for k in range(nk):
                    last = pe.matmul(bank(6 + j % 2)[part:part + HD, g * P:(g + 1) * P], v_rows[:, j + 1 - nk + k, h * HD:(h + 1) * HD],
                                     p_T[u % 2][:, k * P:(k + 1) * P], start=(k == 0), stop=(k == nk - 1))
                last.then_inc(s_PV, 1)

            def turn_sums(j):
                pe.wait_ge(s_rinv, j + 1)
                pe.wait_ge(s_pTc, min(NH * (j + 1) + 3, len(units)))
                pe.transpose(pair[2][0:NH, 0:P], r_inv[:], ident).then_inc(s_rT, 1)

            def spread_sums(j):
                pe.wait_ge(s_rTc, j + 1)
                pe.wait_ge(s_pTc, min(NH * (j + 1) + 4, len(units)))
                if j == 0:
                    pe.wait_ge(s_head, 16)
                for g in range(4):
                    last = pe.matmul(pair[2][:, g * P:(g + 1) * P], head_of[:, g * P:(g + 1) * P], r_T[:], start=True, stop=True)
                last.then_inc(s_rep, 1)

            for u in range(len(units) + 3):
                if u < len(units):
                    scores(u)
                if 2 <= u < len(units) + 2:
                    turn_probs(u - 2)
                if u >= 3:
                    weigh_values(u - 3)
                    if u >= NH + 4 and (u - 3) % NH == 1:
                        turn_sums((u - 3) // NH - 1)
                    if u >= NH + 4 and (u - 3) % NH == 2:
                        spread_sums((u - 3) // NH - 1)
            turn_sums(TT - 1)
            spread_sums(TT - 1)

            pe.wait_ge(s_dve, CT * KC)
            pe.wait_ge(s_Sfree, len(units))
            for half in range(2):
                for t in range(CT):
                    last = pe.matmul(bank(half), ones, uT[:, t, KC - 1 + half * CW:KC - 1 + (half + 1) * CW],
                                     start=(t == 0), stop=(t == CT - 1))
                last.then_inc(s_lnsum, 1)
            for t in range(CT):
                pe.wait_ge(s_lnsq, t + 1)
                for half in range(2):
                    last = pe.matmul(bank(2 + half), ones, ln_sq(t)[:, half * CW:(half + 1) * CW],
                                     start=(t == 0), stop=(t == CT - 1))
                last.then_inc(s_lnvar, 1)

            pe.wait_ge(s_lnhi, CT)
            pe.wait_ge(s_lnlo, CT)
            pe.wait_ge(s_yhi, TT)
            pe.wait_ge(s_ylo, TT)

            def h2_turn(i):
                pe.wait_ge(s_h2, i + 1)
                if i >= 1:
                    pe.wait_ge(s_h2Tc, i)
                for k in range(KT):
                    last = pe.transpose(pair[2][:, k * P:(k + 1) * P], h2r[:, k, i * P:(i + 1) * P], ident)
                last.then_inc(s_h2T, 1)

            def router(i):
                pe.wait_ge(s_h2Tc, i + 1)
                pe.wait_ge(s_rows, 16 * 7)
                for k in range(KT):
                    last = pe.matmul(bank(6)[:, i * E:(i + 1) * E], h2T[:, k, i * P:(i + 1) * P], rw[:, k, :],
                                     start=(k == 0), stop=(k == KT - 1))
                last.then_inc(s_lg, 1)

            for C in (O_CH, O_CH + 1):
                for i in range(TT):
                    m = C * 8 + i
                    dst = tile_begin(m)
                    product(dst, rows_of(op_hi, i), rows_of(op_lo, i), w(w_hi, C), w(w_lo, C), range(KT), True, True,
                            (C, None) if i == 0 else None).then_inc(s_tile, 1)
                    if C > O_CH and i >= 2:
                        h2_turn(i - 2)
                    if C > O_CH and i >= 3:
                        router(i - 3)
            for i in (TT - 2, TT - 1):
                h2_turn(i)
                router(i - 1)
            router(TT - 1)

            pe.wait_ge(s_c2, 16)
            pe.wait_ge(s_mk, 1)
            pe.matmul(bank(0)[:, 0:TT * E], tri, mask[:].rearrange("p i e -> p (i e)"), start=True, stop=True).then_inc(s_rk, 1)
            pe.matmul(bank(1)[:, 0:TT * E], ones, mask[:].rearrange("p i e -> p (i e)"), start=True, stop=True).then_inc(s_rk, 1)
            for i in range(TT):
                last = pe.matmul(bank(2)[0:CAND, 0:1], mask2[:, i, :], ones[:, 0:1], start=(i == 0), stop=(i == TT - 1))
            last.then_inc(s_cn, 1)
            pe.wait_ge(s_cv, 1)
            pe.matmul(bank(3)[0:CAND, 0:2], stri, cand[:, 0:2], start=True, stop=True).then_inc(s_pf, 1)
            pe.wait_ge(s_sl, 1)
            for r, col in enumerate((5, 1, 3, 4)):
                pe.matmul(bank(4)[0:1, r * TABW:(r + 1) * TABW], cand[:, col:col + 1], sel[:], start=True, stop=True)
            pe.matmul(bank(4)[0:1, 4 * TABW:4 * TABW + 2], ones[0:CAND, 0:1], cand[:, 0:2], start=True, stop=True).then_inc(m_done, 1)
            pe.matmul(bank(5)[:, 0:TABW], base_rep[:], sel[:], start=True, stop=True).then_inc(s_tb, 1)


            def find(b, ix, first, B=None, n=None):
                pe.wait_ge(oh_ok, ix + 1)
                if not first or b:
                    pe.wait_ge(idx_ok, ix)
                if not first:
                    pe.wait_ge(x_h, B * 2 + n * 2)
                    pe.wait_ge(x_l, B * 2 + n * 2)
                for t in range(TT):
                    last = pe.matmul(bank(7)[:, 4 * b:4 * b + 4], onehot[:, t, :], rhs[:, t, :], start=(t == 0), stop=(t == TT - 1))
                last.then_inc(i_ps, 1)

            def turn_x(b, ix, before, first, found):
                pe.wait_ge(g_in, ix * 16 + 16)
                pe.wait_ge(idx_ok, found)
                for half in range(2):
                    if not first or b:
                        free = before * 2 + (half + 1 if b else 0)
                        pe.wait_ge(x_h, free)
                        pe.wait_ge(x_l, free)
                    for k in range(4):
                        col = (half * 4 + k) * P
                        last = pe.transpose(bank(6 + half)[:, k * P:(k + 1) * P], xg[b][:, col:col + P], ident)
                    last.then_inc(x_ps, 1)

            pe.wait_ge(s_tab, 1)
            ps = Passes(pe)
            n0 = ps.n0
            for b in range(MAXB):
                def first_block():
                    find(b, b, True)
                if b:
                    with pe.If(n0 > b):
                        first_block()
                else:
                    first_block()
            for b in range(MAXB):
                if b:
                    with pe.If(n0 > b):
                        turn_x(b, b, max(b - 1, 0), True, n0 + 0)
                else:
                    turn_x(b, b, max(b - 1, 0), True, n0 + 0)

            with pe.Fori(0, ps.count) as p:
                n, n2, B = ps.begin(p)
                n_p, w0 = ps.n_p, ps.w0

                def turn_act(c_, b):
                    it = B * 4 + n * c_ + b
                    pe.wait_ge(act_ok, it + 1)
                    pe.wait_ge(aT_h, it + 1)
                    pe.wait_ge(aT_l, it + 1)
                    for k in range(2):
                        last = pe.transpose(bank(5)[:, k * P:(k + 1) * P], act_r[b][:, k * P:(k + 1) * P], ident)
                    last.then_inc(aT_ps, 1)

                def block_product(c_, b):
                    par = (X_CH + c_) % 2
                    dst = bank(u_bank[b][c_ % 2])
                    if b == 0:
                        if c_ < 2:
                            pe.wait_ge(m_free, w0 + n_p * c_ + 2)
                        else:
                            pe.wait_ge(m_free, B * NPC + n * (c_ - 2) + 3)
                    elif c_ == 0:
                        pe.wait_ge(m_free, B * NPC + 2)
                    else:
                        pe.wait_ge(m_free, B * NPC + n * (c_ - 1) + (b + 3))
                    new = (X_CH + c_, p) if b == 0 else None
                    w_of = lambda parts: (lambda k: parts[par][:, k, :])
                    if c_ < 4:
                        if c_ == 0:
                            pe.wait_ge(x_h, B * 2 + (2 * b + 2))
                            pe.wait_ge(x_l, B * 2 + (2 * b + 2))
                        x_of = lambda parts: (lambda k: parts[b][:, k, :])
                        product(dst, x_of(xT_hi), x_of(xT_lo), w_of(w_hi), w_of(w_lo), range(KT), True, True, new).then_inc(m_done, 1)
                        if c_:
                            turn_act(c_ - 1, b)
                    else:
                        a_of = lambda parts: (lambda k: parts[b][:, k, :])
                        args = (a_of(aT_hi), a_of(aT_lo), w_of(w_hi), w_of(w_lo))
                        if c_ == 4:
                            pe.wait_ge(aT_h, B * 4 + n + (b + 2))
                            pe.wait_ge(aT_l, B * 4 + n + (b + 2))
                            product(dst, *args, range(HK), True, False, new)
                            turn_act(3, b)
                            product(dst, *args, range(HK, 6), False, False, new)
                            pe.wait_ge(aT_h, B * 4 + n * 3 + (b + 2))
                            pe.wait_ge(aT_l, B * 4 + n * 3 + (b + 2))
                            product(dst, *args, range(6, KT), False, True).then_inc(m_done, 1)
                        else:
                            product(dst, *args, range(KT), True, True, new).then_inc(m_done, 1)

                for c_ in range(NPC):
                    for b in range(MAXB):
                        if c_ == NPC - 1:
                            with pe.If(n2 > b):
                                turn_x(b, B + n + b, B + n + max(b - 1, 0), False, B + n + n2)
                        if b:
                            with pe.If(n > b):
                                block_product(c_, b)
                        else:
                            block_product(c_, b)
                    if 1 <= c_ <= 4:
                        with pe.If(n2 > c_ - 1):
                            find(c_ - 1, B + n + (c_ - 1), False, B, n)
                ps.end()

        @block.scalar
        def _(act):
            act.wait_ge(s_cols, 1)
            act.activation(c_act[:, 0:8], cols[:, V_C:V_C + 8], ACT.Sigmoid).then_inc(s_csig, 1)
            for i in range(TT):
                act.wait_ge(s_x[i // 4], 16)
                act.activation(pair[2][:], x_rows[:, i, :], ACT.Square, accum_out=stat[:, i:i + 1])
                act.drain()
            act.drain()
            act.activation(stat[:, 8:16], stat[:, 0:8], ACT.Sqrt, bias=eps_col, scale=1.0 / D).then_inc(s_xroot, 1)
            write_hi(act, 0, 0, 16)

            for k in range(KT):
                act.wait_ge(s_xT, k + 1)
                act.wait_ge(s_modc, 1)
                if k >= 2:
                    act.wait_ge(s_hlo, k - 1)
                act.activation(h_full[k % 2][:], pair[k % 2][:], ACT.Identity, bias=mod_col[:, k:k + 1],
                               scale=mod_col[:, 8 + k:9 + k]).then_inc(s_hfull, 1)
                act.wait_ge(s_hfull, k + 1)
                act.activation(op_hi[:, k, :], h_full[k % 2][:], ACT.Copy).then_inc(s_hhi, 1)

            def split(C):
                before_trunk_split(act, C)
                write_hi(act, C % 2, 0, 16 * (C + 1))

            split(1)
            split(2)
            for j in range(8):
                m = GT_CH * 8 + j
                act.wait_ge(s_tile, m + 1)
                if j >= 2:
                    act.wait_ge(s_uz, j - 1)
                act.activation(sig_t[j % 2][:], bank(m % 4), ACT.Sigmoid).then_inc(s_gsig, 1)

            def turned(j):
                act.wait_ge(s_qkT, j + 1)
                i = j % TT
                dst = kT[:, 0:4, i * P:(i + 1) * P] if j < TT else qT[:, 0:4, i * P:(i + 1) * P]
                act.activation(dst, bank(4 + j % 2).rearrange("p (g n) -> p g n", n=P), ACT.Copy).then_inc(s_qkev, 1)

            def roots(j, m):
                act.wait_ge(s_tile, m + 1)
                if j < TT:
                    if j:
                        act.wait_ge(s_qss, j)
                    dst = k_sq[:].rearrange("p (g n) -> p g n", n=P)
                else:
                    dst = q_tmp[:, 4:8, (j - TT) * P:(j - TT + 1) * P]
                act.activation(dst, bank(m % 4).rearrange("p (g n) -> p g n", n=P), ACT.Square).then_inc(s_qsq, 1)
                act.wait_ge(s_qss, j + 1)
                if j < TT:
                    act.activation(sq_root[:], sq_sum[:], ACT.Sqrt, bias=eps_col, scale=1.0 / HD).then_inc(s_qroot, 1)
                else:
                    act.activation(sq_root[:], sq_sum[:], ACT.Sqrt, bias=eps64_col, scale=1.0).then_inc(s_qroot, 1)

            split(3)
            for i in range(TT):
                roots(i, K_CH * 8 + i)
                if i:
                    turned(i - 1)
            split(4)
            turned(TT - 1)
            split(5)
            for i in range(TT):
                roots(TT + i, Q_CH * 8 + i)
                if i:
                    turned(TT + i - 1)
            turned(2 * TT - 1)

            def copy_probs(u):
                nk = min(u // NH, 4) + 1
                act.wait_ge(s_PT, u + 1)
                if u >= 2:
                    act.wait_ge(s_PV, u - 1)
                act.activation(p_T[u % 2][:, 0:nk * P], pair[2][:, 0:nk * P], ACT.Copy).then_inc(s_pTc, 1)

            def copy_sums(j):
                act.wait_ge(s_rT, j + 1)
                act.activation(r_T[:], pair[2][0:NH, 0:P], ACT.Copy).then_inc(s_rTc, 1)

            def outputs_hi(j):
                act.wait_ge(s_y, j + 1)
                act.activation(op_hi[:, 4:8, j * P:(j + 1) * P], y_sb[:].rearrange("p (g n) -> p g n", n=P),
                               ACT.Copy).then_inc(s_yhi, 1)

            for u in range(NH * TT):
                if u >= 2:
                    copy_probs(u - 2)
                j, h = u // NH, u % NH
                nk = min(j, 4) + 1
                act.wait_ge(s_nmx, u + 1)
                act.activation(s_sb[u % 3][:, 0:nk * P], s_sb[u % 3][:, 0:nk * P], ACT.Exp,
                               bias=mx[:, u % 3 * 4 + 2:u % 3 * 4 + 3], accum_out=rsum[:, j % 2 * 8 + h:j % 2 * 8 + h + 1]
                               ).then_inc(s_exp, 1)
                if j and h == 4:
                    copy_sums(j - 1)
                if j and h == 5:
                    outputs_hi(j - 1)
            copy_probs(NH * TT - 2)
            copy_probs(NH * TT - 1)
            copy_sums(TT - 1)
            outputs_hi(TT - 1)
            split(6)

            for t in range(CT):
                act.wait_ge(s_lnc, t + 1)
                if t == 0:
                    act.wait_ge(s_PV, NH * TT)
                if t >= 2:
                    act.wait_ge(s_lnvar, t - 1)
                act.activation(ln_sq(t)[:], uT[:, t, KC - 1:], ACT.Square).then_inc(s_lnsq, 1)
            act.wait_ge(s_lnvar, CT)
            act.activation(ln_r[:], pair[1][:], ACT.Sqrt, bias=eps_col, scale=1.0 / 512).then_inc(s_lnroot, 1)

            def conv_hi(t):
                act.wait_ge(s_lny, t + 1)
                act.activation(op_hi[:, t, :], uT[:, t, KC - 1:], ACT.Copy).then_inc(s_lnhi, 1)

            for t in range(CT):
                act.wait_ge(s_lnz, t + 1)
                if t >= 2:
                    act.wait_ge(s_lny, t - 1)
                act.activation(ln_sig(t)[:], uT[:, t, KC - 1:], ACT.Sigmoid, bias=cols[:, V_LB + t:V_LB + t + 1]).then_inc(s_lnsig, 1)
                if t:
                    conv_hi(t - 1)
            conv_hi(CT - 1)


            def turned_h2(i):
                act.wait_ge(s_h2T, i + 1)
                act.activation(h2T[:, :, i * P:(i + 1) * P], pair[2][:].rearrange("p (k n) -> p k n", n=P), ACT.Copy).then_inc(s_h2Tc, 1)

            for i in range(TT):
                act.wait_ge(s_x2, i + 1)
                act.activation(h2T[:, :, i * P:(i + 1) * P], x2[:, i, :].rearrange("p (k n) -> p k n", n=P), ACT.Square,
                               accum_out=stat[:, i:i + 1])
                act.drain()
                act.activation(stat[:, 8 + i:9 + i], stat[:, i:i + 1], ACT.Sqrt, bias=eps_col, scale=1.0 / D).then_inc(s_x2root, 1)
                if i >= 2:
                    turned_h2(i - 2)
            turned_h2(TT - 2)
            turned_h2(TT - 1)

            act.wait_ge(s_nm, 1)
            act.activation(gex[:], gex[:], ACT.Exp).then_inc(s_gex, 1)

            act.wait_ge(s_tab, 1)
            act.activation(keep[:], pad_id, ACT.Sigmoid).then_inc(aT_h, 1)
            ps = Passes(act)
            n0 = ps.n0
            write_hi(act, X_CH % 2, X_CH % 2, 32)

            def x_hi(b, ix):
                for half in range(2):
                    act.wait_ge(x_ps, ix * 2 + (half + 1))
                    act.activation(xT_hi[b][:, 4 * half:4 * half + 4, :], bank(6 + half).rearrange("p (k n) -> p k n", n=P),
                                   ACT.Copy).then_inc(x_h, 1)

            x_hi(0, 0)
            for b in range(1, MAXB):
                with act.If(n0 > b):
                    x_hi(b, b)
            with act.Fori(0, ps.count) as p:
                act.drain()
                act.activation(keep[:], pad_id, ACT.Sigmoid)
                n, n2, B = ps.begin(p)

                def next_hi(c_, which=(0, 1)):
                    d = (c_ + 1) % NPC
                    more = 0 if c_ < NPC - 1 else 1
                    act.wait_ge(m_done, B * NPC + n * c_ + 1)
                    landed = p * 80 + (80 * more + {0: 32, 2: 64, 4: 80, 1: 112 + 32, 3: 112 + 64, 5: 112 + 80}[d])
                    write_hi(act, (X_CH + d) % 2, (X_CH + d) % 2, landed, which)

                def act_hi(c_, b):
                    act.wait_ge(aT_ps, B * 4 + n * c_ + (b + 1))
                    act.activation(aT_hi[b][:, 2 * c_:2 * c_ + 2, :], bank(5)[:, 0:2 * P].rearrange("p (k n) -> p k n", n=P),
                                   ACT.Copy).then_inc(aT_h, 1)

                def block_step(c_, b):
                    if 1 <= c_ <= 3 or c_ == 4 and b:
                        act_hi(c_ - 1, b)
                    if c_ < 4:
                        act.wait_ge(glu_ok, B * 4 + n * c_ + (b + 1))
                        act.activation(sg[:], ut[:, 0:SQ], ACT.Sigmoid, scale=ALPHA).then_inc(sig_ok, 1)

                for c_ in range(NPC):
                    if c_ == 4:
                        next_hi(c_, (0,))
                        act_hi(3, 0)
                        next_hi(c_, (1,))
                    elif c_ < NPC - 1:
                        next_hi(c_)
                    else:
                        with act.If(n2 > 0):
                            x_hi(0, B + n)
                            next_hi(c_)
                    for b in range(MAXB):
                        if c_ == NPC - 1:
                            if b:
                                with act.If(n2 > b):
                                    x_hi(b, B + n + b)
                        elif b:
                            with act.If(n > b):
                                block_step(c_, b)
                        else:
                            block_step(c_, b)
                ps.end()

        @block.vector
        def _(ve):
            def lo_part(C):
                before_trunk_split(ve, C)
                write_lo(ve, C % 2, 0, C, None, V_KT, s_lo)

            ve.wait_ge(s_vecT, 1)
            ve.tensor_copy(cols[:], bank(6)[:, 0:N_VEC]).then_inc(s_cols, 1)
            ve.wait_ge(s_tapT, 1)
            ve.tensor_copy(taps[:].rearrange("p t k -> p (t k)"), bank(7)[:, 0:CT * KC]).then_inc(s_taps, 1)
            ve.wait_ge(s_csig, 1)
            ve.wait_ge(s_cols, 1)
            ve.tensor_tensor(c_act[:, 8:16], cols[:, V_C:V_C + 8], c_act[:, 0:8], ALU.mult)
            ve.drain()

            def ada_step(n):
                k = n % KT
                if n < KT:
                    ve.wait_ge(s_ada_first[k // 2], 16)
                    tile = ada_first[:, k, :]
                else:
                    ve.wait_ge(s_ada[n % 2], 16 * ((n - KT) // 2 + 1))
                    tile = ada_t[n % 2][:]
                if k == 0:
                    if n:
                        ve.wait_ge(s_modp, 1 if n == KT else 5)
                    ve.tensor_scalar(ada_acc[:], tile, c_act[:, 8:9], None, ALU.mult).then_inc(s_adastep, 1)
                else:
                    ve.wait_ge(s_adastep, n)
                    ve.scalar_tensor_tensor(ada_acc[:], tile, c_act[:, 8 + k:9 + k], ada_acc[:],
                                            ALU.mult, ALU.add).then_inc(s_adastep, 1)

            ve.wait_ge(s_relrow, 16)
            ve.tensor_copy(mx[0:NH, 0:1], rel_rows[:, 256:257])
            ve.memset(rel_rows[:, 257:384], 0.0)
            ve.drain()
            ve.tensor_scalar(rel_rows[:, 0:257], rel_rows[:, 0:257], mx[0:NH, 0:1], None, ALU.subtract).then_inc(s_rel, 1)
            ada_step(0)
            ada_step(1)
            ve.wait_ge(s_xroot, 1)
            ve.reciprocal(stat[:, 0:8], stat[:, 8:16])
            ve.drain()
            for i in range(TT):
                ve.tensor_scalar(x_rows[:, i, :], x_rows[:, i, :], stat[:, i:i + 1], None, ALU.mult).then_inc(s_xn, 1)
            for n in range(2, 8):
                ada_step(n)
            lo_part(0)
            ve.wait_ge(s_modp, 1)
            ve.tensor_tensor(mod_col[:], bank(6)[:, 0:16], cols[:, V_ADA:V_ADA + 16], ALU.add)
            ve.drain()
            ve.scalar_tensor_tensor(mod_col[:, 8:16], mod_col[:, 8:16], 1.0, cols[:, V_G1:V_G1 + 8], ALU.add, ALU.mult).then_inc(s_modc, 1)
            for k in range(KT):
                ve.wait_ge(s_hhi, k + 1)
                ve.tensor_tensor(op_lo[:, k, :], h_full[k % 2][:], op_hi[:, k, :].bitcast(F32), ALU.subtract).then_inc(s_hlo, 1)
            ve.wait_ge(s_hlo, KT)
            ve.memset(uT[:, :, 0:KC - 1], 0.0)

            def mod_values(half):
                ve.wait_ge(s_adab, 16 * (half + 1))
                for j in range(4):
                    m = 4 * half + j
                    ve.wait_ge(s_modp, m + 2)
                    row = mod_row[0:1, j * CW:(j + 1) * CW]
                    ve.tensor_tensor(row, row, bank(6 + m % 2)[0:1, :], ALU.add).then_inc(s_modfree, 1)
                ve.wait_ge(s_modfree, 4 * half + 4)
                ve.sem_inc(s_modr, 1)

            for m in range(8):
                ve.wait_ge(s_tile, m + 1)
                t, half = m // 2, m % 2
                ve.tensor_copy(uT[:, t, KC - 1 + half * CW:KC - 1 + (half + 1) * CW], bank(m % 4)).then_inc(s_tfree, 1)
                if m == 1:
                    lo_part(1)
                if m >= 2:
                    ada_step(KT + m - 2)
            ada_step(2 * KT - 2)
            ada_step(2 * KT - 1)
            mod_values(0)
            for j in range(8):
                m = GT_CH * 8 + j
                t, half = j // 2, j % 2
                ve.wait_ge(s_gsig, j + 1)
                u = uT[:, t, KC - 1 + half * CW:KC - 1 + (half + 1) * CW]
                ve.wait_ge(s_tfree, t * 2 + half + 1)
                ve.tensor_tensor(u, u, sig_t[j % 2][:], ALU.mult).then_inc(s_uz, 1)
                ve.wait_ge(s_uz, j + 1)
                ve.sem_inc(s_tfree, 1)
                if j == 1:
                    lo_part(2)
                ada_step(2 * KT + j)
            mod_values(1)

            conv_done = [0]

            def conv_steps(count):
                for _ in range(count):
                    s = conv_done[0]
                    if s == CT * KC:
                        return
                    ct, tap = s // KC, s % KC
                    src = uT[:, ct, tap:tap + T]
                    w_tap = taps[:, ct, tap:tap + 1]
                    if s:
                        ve.wait_ge(s_dve, s)
                    if tap == 0:
                        ve.tensor_scalar(acc[:], src, w_tap, cols[:, V_CB + ct:V_CB + ct + 1], ALU.mult, ALU.add).then_inc(s_dve, 1)
                    else:
                        dst = acc[:] if tap < KC - 1 else uT[:, ct, KC - 1:]
                        ve.scalar_tensor_tensor(dst, src, w_tap, acc[:], ALU.mult, ALU.add).then_inc(s_dve, 1)
                    conv_done[0] += 1

            ve.wait_ge(s_gain, 32)

            def normalise(j, m):
                ve.wait_ge(s_qsq, j + 1)
                cols_j = slice((j % TT) * P, (j % TT + 1) * P)
                sq = k_sq[:].rearrange("p (g h d) -> p g h d", h=2, d=HD) if j < TT else q_tmp[:, 4:8, cols_j].rearrange("p g (h d) -> p g h d", d=HD)
                ve.tensor_reduce(sq_sum[:].rearrange("p (g h) -> p g h", h=2), sq, AX_X, ALU.add).then_inc(s_qss, 1)
                conv_steps(1)
                ve.wait_ge(s_qroot, j + 1)
                ve.reciprocal(sq_inv[:], sq_root[:])
                if 1 <= j < TT:
                    ve.wait_ge(s_qkT, j)
                ve.drain()
                dst = k_row[:].rearrange("p (g h d) -> p g h d", h=2, d=HD) if j < TT else q_tmp[:, 0:4, cols_j].rearrange("p g (h d) -> p g h d", d=HD)
                ve.tensor_tensor(dst, bank(m % 4).rearrange("p (g h d) -> p g h d", h=2, d=HD),
                                 view(sq_inv[:], [[2, 4], [1, 2], [0, HD]]), ALU.mult).then_inc(s_tfree, 1)
                ve.wait_ge(s_tfree, m + 1)
                ve.tensor_tensor(dst, dst, view(gains[:, 1 if j < TT else 0, :], [[0, 4], [0, 2], [1, HD]]), ALU.mult).then_inc(s_qn, 1)

            for i in range(TT):
                if i == 0:
                    ve.wait_ge(s_modst, 32)
                normalise(i, K_CH * 8 + i)
                conv_steps(2)
                if i == 1:
                    lo_part(3)
            for i in range(TT):
                if i == 0:
                    ve.wait_ge(s_qkT, TT)
                ve.wait_ge(s_tile, V_CH * 8 + i + 1)
                ve.tensor_copy(v_rows[:, i, :], bank((V_CH * 8 + i) % 4)).then_inc(s_tfree, 1)
                if i == 1:
                    lo_part(4)
                conv_steps(3)
            for i in range(TT):
                normalise(TT + i, Q_CH * 8 + i)
                if i == 1:
                    lo_part(5)
                conv_steps(2)

            ve.wait_ge(s_mask, 16)
            ve.wait_ge(s_relld, 16 * NH)
            ve.wait_ge(s_qn, 2 * TT)
            ve.tensor_tensor(near_bias[:, :, 0:64], near_bias[:, :, 0:64], view(masks[:], [[0, NH], [1, 64]], 3 * P), ALU.add)
            ve.drain()

            def invert_sums(j):
                ve.wait_ge(s_exp, NH * (j + 1))
                if j:
                    ve.wait_ge(s_rT, j)
                ve.reciprocal(r_inv[:], rsum[:, j % 2 * 8:j % 2 * 8 + 8]).then_inc(s_rinv, 1)

            def outputs(j):
                ve.wait_ge(s_PV, NH * (j + 1))
                ve.wait_ge(s_rep, j + 1)
                ve.tensor_copy(y_sb[:], bank(6 + j % 2))
                ve.drain()
                ve.tensor_tensor(y_sb[:], y_sb[:], pair[2][:, 0:CW], ALU.mult).then_inc(s_y, 1)

            def outputs_lo(j):
                ve.wait_ge(s_yhi, j + 1)
                cols_j = slice(j * P, (j + 1) * P)
                ve.tensor_tensor(op_lo[:, 4:8, cols_j], y_sb[:].rearrange("p (g n) -> p g n", n=P),
                                 op_hi[:, 4:8, cols_j].bitcast(F32), ALU.subtract).then_inc(s_ylo, 1)

            for u in range(NH * TT):
                j, h = u // NH, u % NH
                nk = min(j, 4) + 1
                nf = max(nk - 2, 0)
                ve.wait_ge(s_S, u + 1)
                if u >= 3:
                    ve.wait_ge(s_PT, u - 2)
                a, near = u % 3 * 4, (nk - nf) * P
                if nf:
                    ve.tensor_tensor_reduce(s_sb[u % 3][:, 0:nf * P], pair[u % 2][:, 0:nf * P], masks[:, (3 - nf) * P:3 * P],
                                            1.0, NEG, ALU.add, ALU.max, mx[:, a:a + 1])
                ve.tensor_tensor_reduce(s_sb[u % 3][:, nf * P:nk * P], pair[u % 2][:, nf * P:nk * P],
                                        view(near_bias[:, h, :], [[-1, near]], near - 1), 1.0, NEG, ALU.add, ALU.max,
                                        mx[:, a + 1:a + 2]).then_inc(s_Sfree, 1)
                ve.wait_ge(s_Sfree, u + 1)
                if nf:
                    ve.tensor_scalar(mx[:, a + 2:a + 3], mx[:, a:a + 1], mx[:, a + 1:a + 2], -1.0, ALU.max, ALU.mult).then_inc(s_nmx, 1)
                else:
                    ve.tensor_scalar(mx[:, a + 2:a + 3], mx[:, a + 1:a + 2], -1.0, None, ALU.mult).then_inc(s_nmx, 1)
                conv_steps(1)
                if j and h == 1:
                    invert_sums(j - 1)
                if j and h == 5:
                    outputs(j - 1)
                if j and h == 6:
                    outputs_lo(j - 1)
            invert_sums(TT - 1)
            outputs(TT - 1)
            outputs_lo(TT - 1)

            ve.wait_ge(s_lnsum, 2)
            for t in range(CT):
                y = uT[:, t, KC - 1:]
                ve.scalar_tensor_tensor(y, pair[0][:], -1.0 / 512, y, ALU.mult, ALU.add).then_inc(s_lnc, 1)
            ve.wait_ge(s_lnroot, 1)
            ve.reciprocal(ln_r[:], ln_r[:])
            ve.drain()

            def conv_y(t):
                y = uT[:, t, KC - 1:]
                ve.wait_ge(s_lnsig, t + 1)
                ve.scalar_tensor_tensor(y, y, cols[:, V_LB + t:V_LB + t + 1], ln_sig(t)[:], ALU.add, ALU.mult).then_inc(s_lny, 1)

            def conv_lo(t):
                ve.wait_ge(s_lnhi, t + 1)
                ve.tensor_tensor(op_lo[:, t, :], uT[:, t, KC - 1:], op_hi[:, t, :].bitcast(F32), ALU.subtract).then_inc(s_lnlo, 1)

            for t in range(CT):
                y = uT[:, t, KC - 1:]
                ve.wait_ge(s_lnsq, t + 1)
                ve.scalar_tensor_tensor(y, y, cols[:, V_LG + t:V_LG + t + 1], ln_r[:], ALU.mult, ALU.mult).then_inc(s_lnz, 1)
                if t >= 1:
                    conv_y(t - 1)
                if t >= 2:
                    conv_lo(t - 2)
            conv_y(CT - 1)
            conv_lo(CT - 2)
            conv_lo(CT - 1)

            ve.wait_ge(s_rows, 16 * 7)

            def add_tile(C, i):
                m, n0_ = C * 8 + i, (C - O_CH) * CW
                ve.wait_ge(s_tile, m + 1)
                ve.tensor_tensor(t_row[i % 2][:], bank(m % 4), g1_row[:, n0_:n0_ + CW], ALU.mult).then_inc(s_tfree, 1)
                ve.wait_ge(s_tfree, m + 1)
                half = x2[:, i, n0_:n0_ + CW]
                ve.wait_ge(s_x2ld[i], 16)
                return ve.tensor_tensor(half, half, t_row[i % 2][:], ALU.add)

            def rows_h2(i):
                ve.wait_ge(s_x2root, i + 1)
                ve.reciprocal(stat[:, i:i + 1], stat[:, 8 + i:9 + i])
                ve.drain()
                h = h2r[:, :, i * P:(i + 1) * P]
                cut = lambda ap: ap.rearrange("p (k n) -> p k n", n=P)
                ve.scalar_tensor_tensor(h, cut(x2[:, i, :]), stat[:, i:i + 1], cut(a2_row[:]), ALU.mult, ALU.mult)
                ve.drain()
                ve.tensor_tensor(h, h, cut(sh2_row[:]), ALU.add).then_inc(s_h2, 1)

            for i in range(TT):
                add_tile(O_CH, i)
                if i == 1:
                    lo_part(6)
            ve.scalar_tensor_tensor(a2_row[:], a2_row[:], 1.0, n2_row[:], ALU.add, ALU.mult)
            ve.drain()
            for i in range(TT):
                add_tile(O_CH + 1, i).then_inc(s_x2, 1)
                if i:
                    rows_h2(i - 1)
            rows_h2(TT - 1)

            ve.wait_ge(s_lg, TT)
            ve.tensor_tensor(lgt[:], bank(6)[:, 0:TT * E].rearrange("p (i e) -> p i e", e=E), view(rb_row[:], [[0, TT], [1, E]]), ALU.add)
            ve.drain()
            for i in range(TT):
                ve.max(top[:, i, :], lgt[:, i, :])
            ve.drain()
            for i in range(TT):
                ve.max_index(top_i[:, i, :], top[:, i, :], lgt[:, i, :])
            ve.drain()
            ve.wait_ge(s_h2st, 16 * TT)
            ve.tensor_tensor(gex[:], top[:, :, 0:TOPK], view(top[:], [[8, TT], [0, TOPK]]), ALU.subtract).then_inc(s_nm, 1)
            ve.tensor_copy(top_f[:], top_i[:])
            ve.wait_ge(s_iota, 16)
            ve.drain()
            per_tile = lambda t, r, step: view(t[:], [[step, TT], [0, E]], r)
            for r in range(TOPK):
                ve.tensor_tensor(hot[:, r], view(iota[:], [[0, TT], [1, E]]), per_tile(top_f, r, 8), ALU.is_equal)
            ve.drain()
            ve.tensor_tensor(mask[:], hot[:, 0], hot[:, 1], ALU.add)
            ve.tensor_tensor(hotg[:], hot[:, 2], hot[:, 3], ALU.add)
            ve.drain()
            ve.tensor_tensor(mask[:], mask[:], hotg[:], ALU.add)
            ve.drain()
            ve.tensor_copy(mask2[:].rearrange("p i (e s) -> p i e s", s=SPLITS),
                           view(mask[:], [[E, TT], [1, E], [0, SPLITS]])).then_inc(s_mk, 1)
            ve.wait_ge(s_gex, 1)
            ve.tensor_reduce(gsum[:], gex[:], AX_X, ALU.add)
            ve.drain()
            ve.reciprocal(ginv[:], gsum[:])
            ve.drain()
            ve.tensor_tensor(gex[:], gex[:], view(ginv[:], [[1, TT], [0, TOPK]]), ALU.mult)
            ve.drain()
            for r in range(TOPK):
                ve.tensor_tensor(hot[:, r], hot[:, r], per_tile(gex, r, TOPK), ALU.mult)
            ve.drain()
            ve.tensor_tensor(gate_te[:], hot[:, 0], hot[:, 1], ALU.add)
            ve.tensor_tensor(hotg[:], hot[:, 2], hot[:, 3], ALU.add)
            ve.drain()
            ve.tensor_tensor(gate_et[:], view(gate_te[:], [[1, E], [E, TT]]), view(hotg[:], [[1, E], [E, TT]]), ALU.add)

            ve.wait_ge(s_c2, 16)
            ve.wait_ge(s_cn, 1)
            ve.tensor_copy(cand[:, 6:7], bank(2)[0:CAND, 0:1])
            ve.tensor_copy(cand[:, 5:6], cand_val[:, 0:1])
            ve.tensor_scalar(base_rep[:], ones[0:CAND, :], cand_val[:, 1:2], None, ALU.mult)
            ve.drain()
            ve.tensor_scalar(cmp[:], thr, cand[:, 6:7], None, ALU.is_lt)
            ve.drain()
            ve.tensor_reduce(cand[:, 1:2], cmp[:], AX_X, ALU.add)
            ve.tensor_copy(cand[:, 0:1], cmp[:, 0:1]).then_inc(s_cv, 1)
            ve.drain()
            ve.wait_ge(s_pf, 1)
            ve.tensor_copy(cand[:, 2:4], bank(3)[0:CAND, 0:2])
            ve.drain()
            ve.tensor_scalar(cand[:, 4:5], cand[:, 3:4], float(NPC), 1.0, ALU.mult, ALU.add)
            ve.tensor_scalar(sel[:], row_m1, cand[:, 2:3], cand[:, 0:1], ALU.is_equal, ALU.mult)
            ve.drain()
            ve.scalar_tensor_tensor(cand[:, 4:5], cand[:, 1:2], 4.0, cand[:, 4:5], ALU.mult, ALU.add).then_inc(s_sl, 1)

            ve.wait_ge(s_rk, 2)
            ve.memset(pre[:, 0, :], 0.0)
            for i in range(1, TT):
                ve.drain()
                ve.tensor_tensor(pre[:, i, :], pre[:, i - 1, :], bank(1)[:, (i - 1) * E:i * E], ALU.add)
            ve.drain()
            ve.tensor_tensor(rank[:], bank(0)[:, 0:TT * E].rearrange("p (i e) -> p i e", e=E), pre[:], ALU.add)
            ve.drain()
            ve.tensor_tensor(rank[:], rank[:], mask[:], ALU.mult)
            ve.drain()
            ve.tensor_scalar(pos_et[:], view(rank[:], [[1, E], [E, TT]]), -1.0, None, ALU.add)
            ve.tensor_copy(rhs[:, :, 0], tok_id)
            ve.tensor_copy(rhs[:, :, 3], ones[:, 0:TT])
            ve.wait_ge(s_tb, 1)
            ve.tensor_copy(pbase[:], bank(5)[:, 0:TABW]).then_inc(m_free, 1)
            ve.tensor_copy(g_idx[:], ones[:, 0:MAXB]).then_inc(m_free, 1)
            ve.tensor_copy(tab[0:1, 0:4 * TABW + 2], bank(4)[0:1, 0:4 * TABW + 2]).then_inc(aT_l, 1)
            ve.wait_ge(aT_l, 1)
            ve.wait_ge(m_free, 2)
            ve.sem_inc(s_tab, 1)

            def slots_of(e_, col):
                ve.tensor_scalar(posr[:], pos_et[:, bass.ds(e_, 1), :].rearrange("p e i -> p (e i)"), col, None, ALU.subtract)
                gates = gate_et[:, bass.ds(e_, 1), :].rearrange("p e i -> p (e i)")
                ve.tensor_copy(rhs[:, :, 1], gates)
                ve.drain()
                ve.tensor_tensor(rhs[:, :, 2], gates, rhs[:, :, 1].bitcast(F32), ALU.subtract)

            def mark(b, ix, first):
                if not first or b:
                    ve.wait_ge(i_ps, ix)
                ve.tensor_scalar(posb[:], posr[:], -float(P * b), None, ALU.add)
                ve.drain()
                ve.tensor_tensor(onehot[:], view(iota[:], [[0, TT], [1, P]]), view(posb[:], [[1, TT], [0, P]]), ALU.is_equal).then_inc(oh_ok, 1)

            def indices(b, ix):
                ve.wait_ge(i_ps, ix + 1)
                ve.tensor_copy(i_sb[:], bank(7)[:, 4 * b:4 * b + 4])
                ve.drain()
                ve.tensor_copy(g_idx[:, b:b + 1], i_sb[:, 0:1])
                ve.tensor_tensor(gt_nxt[:, b:b + 1], i_sb[:, 1:2], i_sb[:, 2:3], ALU.add)
                ve.scalar_tensor_tensor(s_tmp[:, 0:1], i_sb[:, 3:4], neg_pad, pad_id, ALU.mult, ALU.add)
                ve.drain()
                ve.tensor_tensor(s_tmp[:, 1:2], s_tmp[:, 0:1], i_sb[:, 0:1], ALU.add)
                ve.drain()
                ve.tensor_scalar(s_nxt[:, 0, b:b + 1], s_tmp[:, 1:2], 2.0, None, ALU.mult)
                ve.tensor_scalar(s_nxt[:, 1, b:b + 1], s_tmp[:, 1:2], 2.0, 1.0, ALU.mult, ALU.add).then_inc(idx_ok, 1)

            def x_lo(b, ix):
                for half in range(2):
                    ve.wait_ge(x_h, ix * 2 + (half + 1))
                    ve.tensor_tensor(xT_lo[b][:, 4 * half:4 * half + 4, :], bank(6 + half).rearrange("p (k n) -> p k n", n=P),
                                     xT_hi[b][:, 4 * half:4 * half + 4, :].bitcast(F32), ALU.subtract).then_inc(x_l, 1)

            ps = Passes(ve)
            n0 = ps.n0
            e0 = ve.value_load(tab[0:1, 1:2], min_val=0, max_val=E - 1)
            slots_of(e0, pbase[:, 1:2])
            ve.tensor_copy(s_nxt[:].rearrange("p h b -> p (h b)"), ones[:, 0:2 * MAXB])
            ve.tensor_copy(gt_nxt[:], ones[:, 0:MAXB])
            ve.drain()
            mark(0, 0, True)
            indices(0, 0)
            for b in range(1, MAXB):
                with ve.If(n0 > b):
                    mark(b, b, True)
                    indices(b, b)
            write_lo(ve, X_CH % 2, X_CH % 2, X_CH, None, V_KT, s_lo)
            x_lo(0, 0)
            for b in range(1, MAXB):
                with ve.If(n0 > b):
                    x_lo(b, b)

            with ve.Fori(0, ps.count) as p:
                n, n2, B = ps.begin(p)
                e2 = ve.value_load(tab[0:1, bass.ds(p + 2, 1)], min_val=0, max_val=E - 1)

                def add_bias(c_, b):
                    ve.drain()
                    if b == 0:
                        slot = (X_CH + c_) % 3
                        landed = p * (48, 64, 48)[slot] + {0: 32, 3: 64, 1: 32, 4: 48, 2: 32, 5: 48}[c_]
                        ve.wait_ge(s_bias[slot], landed)
                    ve.wait_ge(m_done, B * NPC + n * c_ + (b + 2))
                    src = bank(u_bank[b][c_ % 2])
                    ve.tensor_tensor(ut[:], src, bias[(X_CH + c_) % 3][:], ALU.add).then_inc(m_free, 1)
                    ve.drain()

                def act_lo(c_, b):
                    ve.wait_ge(aT_h, B * 4 + n * c_ + (b + 2))
                    ve.tensor_tensor(aT_lo[b][:, 2 * c_:2 * c_ + 2, :], bank(5)[:, 0:2 * P].rearrange("p (k n) -> p k n", n=P),
                                     aT_hi[b][:, 2 * c_:2 * c_ + 2, :].bitcast(F32), ALU.subtract).then_inc(aT_l, 1)

                def swiglu(c_, b, between=None):
                    add_bias(c_, b)
                    ve.tensor_scalar(ut[:, 0:SQ], ut[:, 0:SQ], LIMIT, None, ALU.min).then_inc(glu_ok, 1)
                    ve.tensor_scalar(ut[:, SQ:], ut[:, SQ:], LIMIT, -LIMIT, ALU.min, ALU.max)
                    if between:
                        between()
                    ve.drain()
                    ve.scalar_tensor_tensor(ut[:, SQ:], ut[:, SQ:], 1.0, ut[:, 0:SQ], ALU.add, ALU.mult)
                    if c_:
                        act_lo(c_ - 1, b)
                    ve.drain()
                    ve.wait_ge(sig_ok, B * 4 + n * c_ + (b + 1))
                    ve.tensor_tensor(act_r[b][:], ut[:, SQ:], sg[:], ALU.mult).then_inc(act_ok, 1)

                def scale_out(c_, b):
                    add_bias(c_, b)
                    iy = B * 2 + n * (c_ - 4) + b
                    ve.wait_ge(y_out, iy * 16 + (16 if b == 0 else 0))
                    h = c_ - 4
                    ve.scalar_tensor_tensor(yst[(b + c_) % 2][:], ut[:], gt_cur[:, b:b + 1], g2_row[:, h * CW:(h + 1) * CW],
                                            ALU.mult, ALU.mult).then_inc(y_ok, 1)

                def block_step(c_, b):
                    if c_ == 4 and b:
                        act_lo(3, b)
                    if c_ < 4:
                        swiglu(c_, b, (lambda: next_lo(c_, (1,))) if b == 0 else None)
                    else:
                        scale_out(c_, b)

                def next_lo(c_, which=(0, 1)):
                    slot = (X_CH + c_ + 1) % 2
                    write_lo(ve, slot, slot, X_CH + c_ + 1, p, V_KT, s_lo, which)

                for c_ in range(NPC):
                    if 2 <= c_:
                        with ve.If(n2 > c_ - 2):
                            indices(c_ - 2, B + n + (c_ - 2))
                    if c_ == 4:
                        act_lo(3, 0)
                    if c_ < NPC - 1:
                        next_lo(c_, (0,))
                    else:
                        with ve.If(n2 > 0):
                            x_lo(0, B + n)
                            next_lo(c_, (0,))
                    for b in range(MAXB):
                        if c_ == NPC - 1 and b:
                            with ve.If(n2 > b):
                                x_lo(b, B + n + b)
                        if b:
                            with ve.If(n > b):
                                block_step(c_, b)
                        else:
                            block_step(c_, b)
                            if c_ == 4:
                                next_lo(c_, (1,))
                            if c_ == NPC - 1:
                                with ve.If(n2 > 0):
                                    next_lo(c_, (1,))
                    if c_ == 0:
                        ve.wait_ge(i_ps, B + n)
                        slots_of(e2, pbase[:, bass.ds(p + 2, 1)])
                        ve.drain()
                    if c_ < 4:
                        with ve.If(n2 > c_):
                            mark(c_, B + n + c_, False)
                    if c_ == 1:
                        ve.wait_ge(y_out, B * 32 + 16)
                        ve.tensor_copy(s_cur[:], s_nxt[:])
                        ve.tensor_copy(gt_cur[:], gt_nxt[:])
                        ve.drain()
                ps.end()


_ARGS = ("x", "c", "ada_w", "ada_b", "norm1_g", "w_in", "conv_w", "conv_b", "conv_ln_g", "conv_ln_b", "q_norm_g",
         "k_norm_g", "rel_bias", "w_out", "norm2_g", "router_w", "router_b", "exp_w1", "exp_b1", "exp_w2", "exp_b2")


def kernel(**inputs):
    import numpy as np
    import concourse.bacc as _bacc
    from concourse.bass_utils import run_bass_kernel_spmd as _run

    nc = _bacc.Bacc("TRN2", target_bir_lowering=False, num_devices=1)
    arrays = {}
    for name in _ARGS:
        a = np.ascontiguousarray(inputs[name])
        arrays["in_" + name] = a if name == "c" else a[0]
    arrays["in_consts"] = make_consts()
    args = [nc.dram_tensor(name, a.shape, F32, kind="ExternalInput").ap() for name, a in arrays.items()]
    rel_ext = nc.dram_tensor("rel_ext", (NH, 384), F32, kind="Internal").ap()
    mod_dram = nc.dram_tensor("mod_dram", (4 * D,), F32, kind="Internal").ap()
    h2_dram = nc.dram_tensor("h2_dram", (T, D), F32, kind="Internal").ap()
    out = nc.dram_tensor("out", (T + P, D), F32, kind="ExternalOutput").ap()
    layer(nc, *args, rel_ext, mod_dram, h2_dram, out)
    r = _run(nc, [arrays], core_ids=[0])
    return np.asarray(r.results[0]["out"])[:T].reshape(1, T, D)
```
